# Optimizing a Trainium2 kernel written in Bass

```python
import math
import jax, jax.numpy as jnp
from jax import lax
import numpy as np

D_MODEL = 1024
BATCH = 1
SEQ = 512
DEPTH = 2

CHUNK = 64
Q_BLOCK = 128
N_A_LAYERS = DEPTH // 2
N_B_LAYERS = DEPTH - N_A_LAYERS
RWKV_HEAD = 64
RWKV_HEADS = D_MODEL // RWKV_HEAD
DECAY_LORA = 64
ICLR_LORA = 64
GATE_LORA = 160
LNX_EPS = 64e-5
MLA_HEADS = 16
QK_NOPE = 64
QK_ROPE = 32
V_HEAD = 64
Q_LORA = 384
KV_LORA = 256
ROPE_THETA = 10000.0
NEG_INF = -1e30
D_FF = 2816
CONV_W = 3
NORM_EPS = 1e-6


def rmsnorm(x, g):
    xf = x.astype(jnp.float32)
    y = xf * lax.rsqrt(jnp.mean(xf * xf, axis=-1, keepdims=True) + NORM_EPS)
    return (y * g.astype(jnp.float32)).astype(x.dtype)

def conv_ffn(x, w_in, conv_w, conv_b, w_out):
    T = x.shape[1]
    gate, up = jnp.split(x @ w_in, 2, axis=-1)
    gp = jnp.pad(gate, ((0, 0), (CONV_W - 1, 0), (0, 0)))
    gc = conv_b
    for j in range(CONV_W):
        gc = gc + gp[:, j:j + T, :] * conv_w[j]
    h = jax.nn.gelu(gc) * up
    return h @ w_out

def _rwkv7_step(S, inp):
    r, w, k, v, a, b = inp
    sa = jnp.einsum('bhvk,bhk->bhv', S, a)
    S = S * w[:, :, None, :] + sa[..., None] * b[:, :, None, :] + v[..., None] * k[:, :, None, :]
    y = jnp.einsum('bhvk,bhk->bhv', S, r)
    return S, y

def rwkv7_time_mix(x, mu, w_rkv, w0, w1, w2, a0, a1, a2, g1, g2, k_k, k_a, r_k, lnx_w, lnx_b, w_o):
    B, T, D = x.shape
    H, N = RWKV_HEADS, RWKV_HEAD
    f32 = jnp.float32
    x_prev = jnp.pad(x, ((0, 0), (1, 0), (0, 0)))[:, :T]
    xx = x_prev - x
    xs = x[None] + xx[None] * mu[:, None, None, :]
    rkv = jnp.einsum('nbtd,nde->nbte', xs[:3], w_rkv)
    r, k, v = rkv[0], rkv[1], rkv[2]
    xw, xa, xg = xs[3], xs[4], xs[5]
    w_log = -jax.nn.softplus(-(w0 + jnp.tanh(xw @ w1) @ w2)) - 0.5
    decay = jnp.exp(-jnp.exp(w_log.astype(f32)))
    a = jax.nn.sigmoid(a0 + (xa @ a1) @ a2)
    g = jax.nn.sigmoid(xg @ g1) @ g2
    kk = (k * k_k).reshape(B, T, H, N).astype(f32)
    kk = kk / jnp.maximum(jnp.sqrt(jnp.sum(kk * kk, axis=-1, keepdims=True)), 1e-12)
    k = k * (1.0 + (a - 1.0) * k_a)
    heads = lambda t: t.reshape(B, T, H, N).astype(f32)
    rh, kh, vh, wh, ah = heads(r), heads(k), heads(v), heads(decay), heads(a)
    seq = tuple(jnp.moveaxis(t, 1, 0) for t in (rh, wh, kh, vh, -kk, kk * ah))
    S0 = jnp.zeros((B, H, N, N), f32)
    _, y = lax.scan(_rwkv7_step, S0, seq)
    y = jnp.moveaxis(y, 0, 1)
    mean = jnp.mean(y, axis=-1, keepdims=True)
    var = jnp.mean(jnp.square(y - mean), axis=-1, keepdims=True)
    yn = ((y - mean) * lax.rsqrt(var + LNX_EPS)).reshape(B, T, D) * lnx_w + lnx_b
    bonus = (jnp.sum(rh * kh * r_k, axis=-1, keepdims=True) * vh).reshape(B, T, D)
    out = ((yn + bonus) * g).astype(x.dtype)
    return out @ w_o

def rope_tables(T):
    inv = 1.0 / (ROPE_THETA ** (jnp.arange(0, QK_ROPE, 2, dtype=jnp.float32) / QK_ROPE))
    ang = jnp.arange(T, dtype=jnp.float32)[:, None] * inv[None, :]
    return jnp.cos(ang), jnp.sin(ang)

def apply_rope(x, cos, sin):
    half = x.shape[-1] // 2
    xf = x.astype(jnp.float32)
    x1, x2 = xf[..., :half], xf[..., half:]
    return jnp.concatenate([x1 * cos - x2 * sin, x1 * sin + x2 * cos], axis=-1).astype(x.dtype)

def mla_attend(q_nope, q_rope, k_nope, k_rope, v):
    B, T, H, _ = q_nope.shape
    nb = T // Q_BLOCK
    scale = 1.0 / math.sqrt(QK_NOPE + QK_ROPE)
    k_chunk = jnp.arange(T) // CHUNK

    def blocks(t):
        return jnp.moveaxis(t.reshape((B, nb, Q_BLOCK) + t.shape[2:]), 1, 0)

    def one_block(args):
        qn, qr, bi = args
        s = jnp.einsum('bqhd,bkhd->bhqk', qn, k_nope) + jnp.einsum('bqhr,bkr->bhqk', qr, k_rope)
        s = s.astype(jnp.float32) * scale
        q_chunk = (bi * Q_BLOCK + jnp.arange(Q_BLOCK)) // CHUNK
        mask = k_chunk[None, :] <= q_chunk[:, None]
        s = jnp.where(mask[None, None], s, NEG_INF)
        p = jax.nn.softmax(s, axis=-1)
        return jnp.einsum('bhqk,bkhd->bqhd', p.astype(v.dtype), v)

    out = lax.map(one_block, (blocks(q_nope), blocks(q_rope), jnp.arange(nb)))
    return jnp.moveaxis(out, 0, 1).reshape(B, T, H, V_HEAD)

def first_inputs(seed: int = 0) -> dict:
    key = jax.random.key(seed)
    ks = jax.random.split(key, 32)
    D, F, H, N = D_MODEL, D_FF, RWKV_HEADS, RWKV_HEAD
    nA, nB = N_A_LAYERS, N_B_LAYERS
    nrm = lambda k, shape, s: jax.random.normal(k, shape, jnp.float32) * s
    return {
        'x': nrm(ks[0], (BATCH, SEQ, D), 1.0),
        'norm_g': 1.0 + nrm(ks[1], (DEPTH, 4, D), 0.05),
        'ffn_w_in': nrm(ks[2], (DEPTH, D, 2 * F), D ** -0.5),
        'ffn_conv_w': nrm(ks[3], (DEPTH, CONV_W, F), CONV_W ** -0.5),
        'ffn_conv_b': nrm(ks[4], (DEPTH, F), 0.01),
        'ffn_w_out': nrm(ks[5], (DEPTH, F, D), F ** -0.5),
        'a_mu': jax.random.uniform(ks[6], (nA, 6, D), jnp.float32),
        'a_w_rkv': nrm(ks[7], (nA, 3, D, D), D ** -0.5),
        'a_w0': jax.random.uniform(ks[8], (nA, D), jnp.float32, minval=-6.5, maxval=-1.5),
        'a_w1': nrm(ks[9], (nA, D, DECAY_LORA), 0.1 * D ** -0.5),
        'a_w2': nrm(ks[10], (nA, DECAY_LORA, D), DECAY_LORA ** -0.5),
        'a_a0': nrm(ks[11], (nA, D), 0.1),
        'a_a1': nrm(ks[12], (nA, D, ICLR_LORA), 0.1 * D ** -0.5),
        'a_a2': nrm(ks[13], (nA, ICLR_LORA, D), ICLR_LORA ** -0.5),
        'a_g1': nrm(ks[14], (nA, D, GATE_LORA), D ** -0.5),
        'a_g2': nrm(ks[15], (nA, GATE_LORA, D), GATE_LORA ** -0.5),
        'a_k_k': 0.85 + nrm(ks[16], (nA, D), 0.05),
        'a_k_a': 1.0 + nrm(ks[17], (nA, D), 0.05),
        'a_r_k': nrm(ks[18], (nA, H, N), 0.1),
        'a_lnx_w': 1.0 + nrm(ks[19], (nA, D), 0.05),
        'a_lnx_b': nrm(ks[20], (nA, D), 0.01),
        'a_w_o': nrm(ks[21], (nA, D, D), D ** -0.5),
        'kv_norm_g': 1.0 + nrm(ks[22], (D,), 0.05),
        'kv_w_down': nrm(ks[23], (D, KV_LORA + QK_ROPE), D ** -0.5),
        'kv_a_norm_g': 1.0 + nrm(ks[24], (KV_LORA,), 0.05),
        'kv_w_up': nrm(ks[25], (KV_LORA, MLA_HEADS * (QK_NOPE + V_HEAD)), KV_LORA ** -0.5),
        'q_w_down': nrm(ks[26], (nB, D, Q_LORA), D ** -0.5),
        'q_norm_g': 1.0 + nrm(ks[27], (nB, Q_LORA), 0.05),
        'q_w_up': nrm(ks[28], (nB, Q_LORA, MLA_HEADS * (QK_NOPE + QK_ROPE)), Q_LORA ** -0.5),
        'o_w': nrm(ks[29], (nB, MLA_HEADS * V_HEAD, D), (MLA_HEADS * V_HEAD) ** -0.5),
    }

def first_block(x, norm_g, ffn_w_in, ffn_conv_w, ffn_conv_b, ffn_w_out,
              a_mu, a_w_rkv, a_w0, a_w1, a_w2, a_a0, a_a1, a_a2, a_g1, a_g2,
              a_k_k, a_k_a, a_r_k, a_lnx_w, a_lnx_b, a_w_o,
              kv_norm_g, kv_w_down, kv_a_norm_g, kv_w_up,
              q_w_down, q_norm_g, q_w_up, o_w):
    B, T, _ = x.shape
    cos, sin = rope_tables(T)
    k_nope = k_rope = v_sh = None
    for layer in range(DEPTH):
        h = rmsnorm(x, norm_g[layer, 0])
        if layer < N_A_LAYERS:
            i = layer
            m = rwkv7_time_mix(h, a_mu[i], a_w_rkv[i], a_w0[i], a_w1[i], a_w2[i],
                               a_a0[i], a_a1[i], a_a2[i], a_g1[i], a_g2[i],
                               a_k_k[i], a_k_a[i], a_r_k[i], a_lnx_w[i], a_lnx_b[i], a_w_o[i])
        else:
            if layer == N_A_LAYERS:
                down = rmsnorm(x, kv_norm_g) @ kv_w_down
                c_kv = rmsnorm(down[..., :KV_LORA], kv_a_norm_g)
                k_rope = apply_rope(down[..., KV_LORA:], cos, sin)
                up = (c_kv @ kv_w_up).reshape(B, T, MLA_HEADS, QK_NOPE + V_HEAD)
                k_nope, v_sh = up[..., :QK_NOPE], up[..., QK_NOPE:]
            j = layer - N_A_LAYERS
            c_q = rmsnorm(h @ q_w_down[j], q_norm_g[j])
            q = (c_q @ q_w_up[j]).reshape(B, T, MLA_HEADS, QK_NOPE + QK_ROPE)
            q_nope = q[..., :QK_NOPE]
            q_rope = apply_rope(q[..., QK_NOPE:], cos[:, None, :], sin[:, None, :])
            o = mla_attend(q_nope, q_rope, k_nope, k_rope, v_sh)
            m = o.reshape(B, T, MLA_HEADS * V_HEAD) @ o_w[j]
        x = x + rmsnorm(m, norm_g[layer, 1])
        f = conv_ffn(rmsnorm(x, norm_g[layer, 2]), ffn_w_in[layer], ffn_conv_w[layer],
                     ffn_conv_b[layer], ffn_w_out[layer])
        x = x + rmsnorm(f, norm_g[layer, 3])
    return x


DEPTH_2 = 1

POOL_WIDTH = 512
POOL_WINDOWS = (2, 4, 8, 16)
N_POOL_GROUPS = len(POOL_WINDOWS)
POOL_GROUP = POOL_WIDTH // N_POOL_GROUPS
N_Q_HEADS = 8
N_KV_HEADS = 2
HEAD_DIM = 64
Q_GROUP = N_Q_HEADS // N_KV_HEADS
Q_WIDTH = N_Q_HEADS * HEAD_DIM
KV_WIDTH = N_KV_HEADS * HEAD_DIM
WINDOW = 128
BLOCK = 128
N_BRANCHES = 2
IN_WIDTH = POOL_WIDTH + Q_WIDTH + 2 * KV_WIDTH + N_BRANCHES * D_MODEL
D_FF_2 = ((8 * D_MODEL + 3 * 256 - 1) // (3 * 256)) * 256
EPS = 1e-6


def rms_norm(x, gain):
    xf = x.astype(jnp.float32)
    y = xf * lax.rsqrt(jnp.mean(xf * xf, axis=-1, keepdims=True) + EPS)
    return (y * gain.astype(jnp.float32)).astype(x.dtype)

def alibi_slopes():
    h = jnp.arange(1, N_Q_HEADS + 1, dtype=jnp.float32)
    return jnp.exp2(-8.0 * h / N_Q_HEADS)

def multiscale_pool(z, w_group, scale):
    B, S, _ = z.shape
    zf = z.astype(jnp.float32)
    cs = jnp.pad(jnp.cumsum(zf, axis=1), ((0, 0), (1, 0), (0, 0)))
    t = jnp.arange(S)
    outs = []
    for g, w in enumerate(POOL_WINDOWS):
        sl = slice(g * POOL_GROUP, (g + 1) * POOL_GROUP)
        lo = jnp.clip(t - w // 2, 0, S)
        hi = jnp.clip(t + w // 2, 0, S)
        csg = cs[..., sl]
        count = (hi - lo).astype(jnp.float32)[None, :, None]
        mean = (csg[:, hi] - csg[:, lo]) / count
        outs.append(mean - zf[..., sl])
    d = jnp.stack(outs, axis=2).astype(z.dtype)
    y = jnp.einsum("bsgc,gcd->bsgd", d, w_group).reshape(B, S, POOL_WIDTH)
    return y * scale

def band_blocks(t, nb):
    B = t.shape[0]
    t = jnp.pad(t, ((0, 0), (BLOCK, BLOCK), (0, 0), (0, 0)))
    t = t.reshape(B, nb + 2, BLOCK, N_KV_HEADS, HEAD_DIM)
    return jnp.concatenate([t[:, :-2], t[:, 1:-1], t[:, 2:]], axis=2)

def windowed_gqa(q, k, v, sink):
    B, S, _ = q.shape
    nb = S // BLOCK
    qb = (q * (HEAD_DIM ** -0.5)).reshape(B, nb, BLOCK, N_KV_HEADS, Q_GROUP, HEAD_DIM)
    kb = band_blocks(k.reshape(B, S, N_KV_HEADS, HEAD_DIM), nb)
    vb = band_blocks(v.reshape(B, S, N_KV_HEADS, HEAD_DIM), nb)
    scores = jnp.einsum("bnqhgd,bnkhd->bnhgqk", qb, kb).astype(jnp.float32)
    a = jnp.arange(BLOCK)[:, None]
    c = jnp.arange(3 * BLOCK)[None, :]
    absdist = jnp.abs(a - c + BLOCK)
    kpos = (jnp.arange(nb)[:, None] - 1) * BLOCK + jnp.arange(3 * BLOCK)[None, :]
    kvalid = (kpos >= 0) & (kpos < S)
    mask = (absdist <= WINDOW)[None, :, :] & kvalid[:, None, :]
    slopes = alibi_slopes().reshape(N_KV_HEADS, Q_GROUP)[:, :, None, None]
    scores = scores - slopes * absdist.astype(jnp.float32)
    scores = jnp.where(mask[None, :, None, None, :, :], scores, -jnp.inf)
    sink_l = sink.astype(jnp.float32).reshape(N_KV_HEADS, Q_GROUP)[:, :, None, None]
    m = jnp.maximum(jnp.max(scores, axis=-1, keepdims=True), sink_l)
    p = jnp.exp(scores - m)
    denom = jnp.sum(p, axis=-1, keepdims=True) + jnp.exp(sink_l - m)
    p = (p / denom).astype(v.dtype)
    out = jnp.einsum("bnhgqk,bnkhd->bnqhgd", p, vb)
    return out.reshape(B, S, Q_WIDTH)

def second_inputs(seed: int = 0) -> dict:
    key = jax.random.key(seed)
    ks = jax.random.split(key, 16)
    f32 = jnp.float32

    def dense(k, shape, fan_in):
        return jax.random.normal(k, shape, f32) * (fan_in ** -0.5)

    def gain(k, shape):
        return 1.0 + 0.05 * jax.random.normal(k, shape, f32)

    return {
        "x": jax.random.normal(ks[0], (BATCH, SEQ, D_MODEL), f32),
        "norm_mix": gain(ks[1], (DEPTH_2, D_MODEL)),
        "w_in": dense(ks[2], (DEPTH_2, D_MODEL, IN_WIDTH), D_MODEL),
        "w_pool_group": dense(ks[3], (DEPTH_2, N_POOL_GROUPS, POOL_GROUP, POOL_GROUP), POOL_GROUP),
        "pool_scale": gain(ks[4], (DEPTH_2, POOL_WIDTH)),
        "sink": 0.5 * jax.random.normal(ks[5], (DEPTH_2, N_Q_HEADS), f32),
        "w_pool_branch": dense(ks[6], (DEPTH_2, POOL_WIDTH, D_MODEL), POOL_WIDTH),
        "w_attn_branch": dense(ks[7], (DEPTH_2, Q_WIDTH, D_MODEL), Q_WIDTH),
        "w_out": dense(ks[8], (DEPTH_2, D_MODEL, D_MODEL), D_MODEL),
        "norm_ffn": gain(ks[9], (DEPTH_2, D_MODEL)),
        "w_ffn_gate": dense(ks[10], (DEPTH_2, D_MODEL, D_FF_2), D_MODEL),
        "w_ffn_up": dense(ks[11], (DEPTH_2, D_MODEL, D_FF_2), D_MODEL),
        "w_ffn_down": dense(ks[12], (DEPTH_2, D_FF_2, D_MODEL), D_FF_2),
        "norm_final": gain(ks[13], (D_MODEL,)),
    }

def second_block(x, norm_mix, w_in, w_pool_group, pool_scale, sink, w_pool_branch,
              w_attn_branch, w_out, norm_ffn, w_ffn_gate, w_ffn_up, w_ffn_down, norm_final):
    splits = [POOL_WIDTH,
              POOL_WIDTH + Q_WIDTH,
              POOL_WIDTH + Q_WIDTH + KV_WIDTH,
              POOL_WIDTH + Q_WIDTH + 2 * KV_WIDTH,
              POOL_WIDTH + Q_WIDTH + 2 * KV_WIDTH + D_MODEL]
    h = x
    for l in range(DEPTH_2):
        u = rms_norm(h, norm_mix[l])
        proj = u @ w_in[l]
        z_pool, q, k, v, g_pool, g_attn = jnp.split(proj, splits, axis=-1)
        y_pool = multiscale_pool(z_pool, w_pool_group[l], pool_scale[l]) @ w_pool_branch[l]
        y_attn = windowed_gqa(q, k, v, sink[l]) @ w_attn_branch[l]
        merged = jax.nn.sigmoid(g_pool) * y_pool + jax.nn.sigmoid(g_attn) * y_attn
        h = h + merged @ w_out[l]
        u = rms_norm(h, norm_ffn[l])
        h = h + (jax.nn.silu(u @ w_ffn_gate[l]) * (u @ w_ffn_up[l])) @ w_ffn_down[l]
    return rms_norm(h, norm_final)


def setup_inputs(seed=0):
    out = dict(first_inputs(seed))
    for name, value in second_inputs(seed + 1).items():
        if name != "x":
            out[name + "_2"] = value
    return out


def reference(
    x, norm_g, ffn_w_in, ffn_conv_w, ffn_conv_b, ffn_w_out, a_mu, a_w_rkv, a_w0, a_w1, a_w2,
    a_a0, a_a1, a_a2, a_g1, a_g2, a_k_k, a_k_a, a_r_k, a_lnx_w, a_lnx_b, a_w_o, kv_norm_g,
    kv_w_down, kv_a_norm_g, kv_w_up, q_w_down, q_norm_g, q_w_up, o_w, norm_mix_2, w_in_2,
    w_pool_group_2, pool_scale_2, sink_2, w_pool_branch_2, w_attn_branch_2, w_out_2, norm_ffn_2,
    w_ffn_gate_2, w_ffn_up_2, w_ffn_down_2, norm_final_2,
):
    x = first_block(
        x, norm_g, ffn_w_in, ffn_conv_w, ffn_conv_b, ffn_w_out, a_mu, a_w_rkv, a_w0, a_w1, a_w2,
        a_a0, a_a1, a_a2, a_g1, a_g2, a_k_k, a_k_a, a_r_k, a_lnx_w, a_lnx_b, a_w_o, kv_norm_g,
        kv_w_down, kv_a_norm_g, kv_w_up, q_w_down, q_norm_g, q_w_up, o_w,
    )
    return second_block(
        x, norm_mix_2, w_in_2, w_pool_group_2, pool_scale_2, sink_2, w_pool_branch_2,
        w_attn_branch_2, w_out_2, norm_ffn_2, w_ffn_gate_2, w_ffn_up_2, w_ffn_down_2,
        norm_final_2,
    )


_drawn_inputs = setup_inputs


def setup_inputs(seed=0):
    import zlib

    import numpy as np

    out = dict(_drawn_inputs(seed))
    spreads = {}
    factors = {'ffn_conv_b': 6.281,
     'a_w1': 8.0,
     'a_w2': 8.0,
     'norm_mix_2': 4.552,
     'pool_scale_2': 5.578,
     'sink_2': 64.0,
     'norm_ffn_2': 2.993}
    for name, (base, spread) in spreads.items():
        noise = np.random.default_rng([zlib.crc32(name.encode()), seed]).standard_normal(out[name].shape)
        drawn = base * np.exp(spread * noise) if base else spread * noise
        out[name] = __import__('jax').numpy.asarray(drawn.astype(out[name].dtype))
    for name, factor in factors.items():
        out[name] = (out[name] * factor).astype(out[name].dtype)
    return out
```

```python
from contextlib import ExitStack

import numpy as np

import concourse.bass as bass
from concourse import mybir

F32 = mybir.dt.float32
F32R = mybir.dt.float32r
ALU = mybir.AluOpType
ACT = mybir.ActivationFunctionType
AX = mybir.AxisListType

P = 128
T = 512
D = 1024
DT = D // P
TT = T // P
HEAD = 64
CHUNK = 64
NCH = T // CHUNK
FF = 2816
FT = FF // P
PARTS = (8, 8, 6)
SLOTS = 4
LEAD = 2
NORM_EPS = 1e-6
LNX_EPS = 64e-5
DECAY_C = float(np.exp(-0.5))
MLA_HEADS = 16
NOPE, ROPE = 64, 32
QK = NOPE + ROPE
MLA_SCALE = float(QK ** -0.5)
G_REST = 160 - P
POOL_W = (2, 4, 8, 16)
PAD = 8
LEVELS = 5
NEG = -1e30


def columns(layout):
    at, out = 0, {}
    for name, n in layout:
        out[name] = (at, n)
        at += n
    return out, at


VEC, NVEC = columns([("norm_g", 64), ("mu", 48), ("kv_norm", 8), ("kv_a_norm", 2), ("q_norm", 3), ("norm_mix", 8),
                     ("norm_ffn", 8), ("norm_final", 8), ("pool_scale", 4), ("sink", 8), ("lnx_w", 8), ("lnx_b", 8), ("conv", 2 * FT * 4)])
CONST, NCONST = columns([("eps", 1), ("lnx_eps", 1), ("slope", 8), ("ones", P), ("head_ones", P), ("head_mean", P),
                         ("ident", P), ("ident_half", HEAD), ("strict", P), ("incl", P), ("level", (LEVELS + 1) * P),
                         ("scan", T)])
LATE, NLATE = columns([("cossin", T), ("absdist", 3 * P), ("inv_count", 4 * 2 * PAD), ("mask_q", P), ("mask_k", P)])
PREP_STEPS = ("omka", "kclamp", "kinv0", "kinv1", "kinv2", "kinv3", "kfac", "knew", "kk", "btok")
TILE_VECS = ("w0", "a0", "k_k", "k_a", "r_k")
SCORES = ((0, 0), (0, 1), (0, 2), (1, 0), (1, 1), (1, 2), (1, 3), (0, 3))

def step(j, name, steps=PREP_STEPS):
    return j * len(steps) + (steps.index(name) + 1)


def phase_list():
    out = [("lora", 4, (8,) * 4), ("r", 8, (8,) * 4), ("k", 8, (8,) * 4), ("v", 8, (8,) * 4), ("w_o", 8, (8,) * 4)]

    def ffn(tag):
        for p, kt in enumerate(PARTS):
            out.append((f"{tag}gu{p}", 2 * kt, (8,) * 4))
            out.append((f"{tag}dn{p}", 8, (kt,) * 4))
    ffn("f0")
    out += [("kvd", 3, (8,) * 4), ("qd", 3, (8,) * 4), ("heads", 32, (2, 3, 2, 3)), ("o_w", 8, (8,) * 4)]
    ffn("f1")
    out += [("in", 10, (8,) * 4), ("mix", 32, (8, 8, 4, 4)), ("out", 8, (8,) * 4)]
    ffn("f2")
    return out


PHASES = phase_list()
ORDER = [p[0] for p in PHASES]
UNITS = {p[0]: p[1] for p in PHASES}
KS = {p[0]: p[2] for p in PHASES}
BY_SLOT = ("heads", "mix")
STRAIGHT = ("in",)
FENCES = ("v",)
FLAT = [(name, u) for name in ORDER for u in range(UNITS[name])]


def starts():
    counts, out = [0] * SLOTS, {}
    for name in ORDER:
        out[name] = tuple(counts)
        for s in range(SLOTS):
            counts[s] += (UNITS[name] - s + SLOTS - 1) // SLOTS
    out["end"] = tuple(counts)
    return out


START = starts()
FOLLOWS = dict(zip(ORDER, ORDER[1:] + ["end"]))

NORM_AT = {}
_first = 0
for _i, (_name, _n) in enumerate([("n_mix", 8), ("n_wo", 8), ("n_f0", 8), ("n_f0out", 8), ("n_mla", 8), ("n_ckv", 2),
                                  ("n_cq", 3), ("n_ow", 8), ("n_f1", 8), ("n_f1out", 8), ("n_in", 8), ("n_f2", 8),
                                  ("n_final", 8)]):
    NORM_AT[_name] = (_i, _first, _n)
    _first += _n
NORMED_AT, _first = {}, 0
for _name, _n in (("f0", 8), ("kv", 8), ("q", 8), ("ckv", 2), ("cq", 3), ("f1", 8), ("in", 8), ("f2", 8)):
    NORMED_AT[_name] = (_first, _n)
    _first += _n
RESID_AT = {"w_o": 0, "f0": 8, "o_w": 16, "f1": 24}
HIDDEN_AT = {"f0": 0, "f1": FT, "f2": 2 * FT}
MIXES = {"w1": (0, 3, "a"), "a1": (1, 4, "b"), "g1": (2, 5, "a"), "r": (3, 0, "b"), "k": (4, 1, "a"), "v": (5, 2, "b")}


def over_units(eng, name, body, ahead=None):
    n, first = UNITS[name], START[name]

    def one(i, r):
        if ahead is not None:
            v = r + LEAD
            ahead(name, i + v // SLOTS, v % SLOTS, first[v % SLOTS] + i + v // SLOTS)
        body(i, r, first[r] + i)

    main = 0 if name in STRAIGHT else max(n - (LEAD if ahead is not None else 0), 0) // SLOTS
    if main > 1:
        with eng.Fori(0, main) as i:
            for r in range(SLOTS):
                one(i, r)
    elif main == 1:
        for r in range(SLOTS):
            one(0, r)
    for u in range(SLOTS * main, n):
        if ahead is not None:
            g = FLAT.index((name, u)) + LEAD
            if g < len(FLAT) and (FLAT[g][0] == name or name not in FENCES):
                ahead_of(ahead, g)
        body(u // SLOTS, u % SLOTS, first[u % SLOTS] + u // SLOTS)


def ahead_of(ahead, g):
    name, u = FLAT[g]
    ahead(name, u // SLOTS, u % SLOTS, START[name][u % SLOTS] + u // SLOTS)


def start_ahead(ahead, name):
    for g in range(FLAT.index((name, 0)), FLAT.index((name, 0)) + LEAD):
        ahead_of(ahead, g)


def build(nc, dram, out_d):
    with ExitStack() as ctx:
        cursor = [16512]

        def place(size):
            at = cursor[0]
            cursor[0] += (size + 31) // 32 * 32
            return at

        def at(name, shape, offset, dt=F32):
            return nc.alloc_sbuf_tensor_at(name, list(shape), dt, offset=offset)

        ROW = T * 4
        X0, M0, A0, B0, R0, W0 = (place(n) for n in (8 * ROW, 8 * ROW + 32, 16 * ROW, 16 * ROW, 16 * ROW, 24 * ROW))

        x = at("x", [P, DT, T], X0)
        m = at("m", [P, DT, T], M0)
        opnd = {n: (at(f"{n}_hi", [P, DT, T], o, F32R), at(f"{n}_lo", [P, DT, T], o + 8 * ROW, F32R))
                for n, o in (("a", A0), ("b", B0), ("c", R0))}
        raw = [at(f"w_raw{s}", [P, 8, P], W0 + 4096 * s) for s in range(SLOTS)]
        w_hi = [at(f"w_hi{s}", [P, 8, P], W0 + 16384 + 4096 * s, F32R) for s in range(SLOTS)]
        w_lo = [at(f"w_lo{s}", [P, 8, P], W0 + 32768 + 4096 * s, F32R) for s in range(SLOTS)]
        consts = at("consts", [P, NCONST], place(NCONST * 4))
        L0 = place(NLATE * 4)
        late = at("late", [P, NLATE], L0)
        vecs = at("vecs", [P, NVEC], place(NVEC * 4))
        omu = at("one_minus_mu", [P, 48], place(192))
        tmp = [at(f"tmp{i}", [P, T], place(ROW)) for i in range(2)]
        sq = [at(f"sq{i}", [P, T], place(ROW)) for i in range(2)]
        STD0 = place(ROW)
        std = at("std", [P, T], STD0)
        rstd = at("rstd", [P, T], place(ROW))
        G0 = place(ROW + 32)
        G1 = place(ROW)
        gpad, gconv = at("gpad", [P, T + 2], G0), at("gconv", [P, T], G1)
        gact = sq

        def const(name, rows=slice(0, P), lo=0, hi=None):
            a, n = CONST[name] if name in CONST else LATE[name]
            return (consts if name in CONST else late)[rows, a + lo:a + (n if hi is None else hi)]

        def column(buf, a, j, rows=slice(0, P)):
            return buf[rows, a + j:a + j + 1] if isinstance(j, int) else buf[rows, bass.ds(j + a, 1)]

        def vec(name, j, rows=slice(0, P)):
            return column(vecs, VEC[name][0], j, rows)

        def tile(buf, j, lo=0, hi=T, rows=slice(0, P)):
            if isinstance(j, int):
                return buf[rows, j, lo:hi]
            return buf[rows, bass.ds(j, 1), lo:hi].rearrange("p a t -> p (a t)")

        hp = at("hp", [P, DT, T + 1], M0)
        r_t, k_t, v_t = at("r_t", [P, DT, T], R0), at("k_t", [P, DT, T], R0 + 8 * ROW), at("v_t", [P, DT, T], X0)
        z_t = at("z_t", [P, DT, T], B0)
        lora_wa, lora_g0 = at("lora_wa", [P, T], L0), at("lora_g0", [P, T], L0 + ROW)
        lora_g1 = at("lora_g1", [G_REST, T], STD0)
        rows_free = iter([M0 + ROW * i for i in range(8)] + [A0 + ROW * i for i in range(16)]
                         + [B0 + ROW * i for i in range(8, 16)] + [W0 + ROW * i for i in range(24)])

        def scratch(name, shape=(P, T)):
            return at("rw_" + name, shape, next(rows_free))

        (sig_w, cum, inv_decay, a_gate, k_sq, k_norm, k_clamp, k_inv, kk, a_dec, b_tok, b_dec, k_fac, k_new,
         k_dec, r_dec, rkr, v_s) = (scratch(n) for n in (
             "sig_w cum inv_decay a_gate k_sq k_norm k_clamp k_inv kk a_dec b_tok b_dec k_fac k_new k_dec "
             "r_dec rkr v_s").split())
        a_nat, b_nat, k_nat, v_nat, x_nat, w_nat, u_nat = (
            scratch(n, (P, TT, P)) for n in "a_nat b_nat k_nat v_nat x_nat w_nat u_nat".split())
        ab, rb, ak, rk, inv, inv_t, off, prod = (
            [scratch(f"{n}{p}", (P, TT, P)) for p in range(2)] for n in "ab rb ak rk inv inv_t off prod".split())
        trans, r_hat, states = scratch("trans"), scratch("r_hat"), scratch("states", (P, NCH, HEAD))
        gain = scratch("gain", (P, NCH, HEAD))
        y_t, y_dev, y_sq, y_std, y_rstd, y_n = sig_w, cum, k_sq, k_norm, k_clamp, k_inv
        decay = at("decay", [P, NCH, CHUNK + 1], G0)
        lora2 = at("lora2", [P, 3, P], G1)
        tvec = at("tvec", [P, len(TILE_VECS) + 1], place(32))

        down = at("down", [P, 5, T], M0)
        cq = (at("cq_hi", [P, 3, T], R0, F32R), at("cq_lo", [P, 3, T], R0 + 3 * ROW, F32R))
        ckv = (at("ckv_hi", [P, 2, T], R0 + 6 * ROW, F32R), at("ckv_lo", [P, 2, T], R0 + 8 * ROW, F32R))
        kf = [at(f"kf{p}", [P, T], R0 + (10 + p) * ROW) for p in range(2)]
        qf = [at(f"qf{p}", [P, T], R0 + (12 + p) * ROW) for p in range(2)]
        v_tr = [at(f"v_tr{p}", [P, T], R0 + (14 + p) * ROW) for p in range(2)]
        v_tok = [at(f"v_tok{p}", [P, TT, HEAD], B0 + 1024 * p) for p in range(2)]
        prob = [at(f"prob{i}", [P, T], B0 + (1 + i) * ROW) for i in range(4)]
        prob_t = [at(f"prob_t{p}", [P, TT, T], B0 + (5 + 4 * p) * ROW) for p in range(2)]
        stat = at("stat", [P, 64], place(256))
        ends = at("ends", [P, NCH, 1], place(32))

        ZW = T + 2 * PAD
        R1 = R0 + 6 * ROW + 4 * ZW * 4
        q2, k2, v2 = at("q2", [P, 4, T], R0), at("k2", [P, T], R0 + 4 * ROW), at("v2", [P, T], R0 + 5 * ROW)
        z2 = at("z2", [P, 4, ZW], R0 + 6 * ROW)
        pool_w = at("pool_w", [P, 4, P], R1)
        q2s = at("q2s", [P, T], R1 + ROW)
        yp = (at("yp_hi", [P, 4, T], B0, F32R), at("yp_lo", [P, 4, T], B0 + 4 * ROW, F32R))
        ya = (at("ya_hi", [P, 4, T], B0 + 8 * ROW, F32R), at("ya_lo", [P, 4, T], B0 + 12 * ROW, F32R))
        win = [at(f"win{i}", [P, ZW], M0 + ZW * 4 * i) for i in range(2)]
        dev2 = at("dev2", [P, T], M0 + 2 * ZW * 4)
        v2n = at("v2n", [P, TT, P], M0 + 7680)
        s2 = [at(f"s2{p}", [P, 3 * P], M0 + 9728 + 1536 * p) for p in range(2)]
        p2t = [at(f"p2t{p}", [P, 3, P], M0 + 12800 + 1536 * p) for p in range(2)]
        gates = [at(f"gates{i}", [P, T], M0 + ROW * i) for i in range(4)]
        assert cursor[0] <= 229344, cursor[0]

        bank = [ctx.enter_context(nc.psum_tensor(f"bank{b}", [P, T], F32)) for b in range(8)]

        def signals(text):
            return [ctx.enter_context(nc.semaphore(n)) for n in text.split()]

        w_loaded, w_high, w_split, unit_done, bank_free = (
            [ctx.enter_context(nc.semaphore(f"{n}{s}")) for s in range(SLOTS)]
            for n in ("w_loaded", "w_high", "w_split", "unit_done", "bank_free"))
        (const_loaded, x_loaded, x_back, sq_ready, sq_used, sum_ready, std_ready, rstd_ready, omu_ready) = signals(
            "const_loaded x_loaded x_back sq_ready sq_used sum_ready std_ready rstd_ready omu_ready")
        (resid_tmp, x_ready, normed_tmp, normed_high, normed_low, h_ready, out_ready, out_stored) = signals(
            "resid_tmp x_ready normed_tmp normed_high normed_low h_ready out_ready out_stored")
        (mix_base, mix_tmp, mix_high, mix_low, zeroed) = signals(
            "mix_base mix_tmp mix_high mix_low zeroed")
        (gate_padded, conv0, conv_done, gate_act, hid_tmp, hid_high) = signals(
            "gate_padded conv0 conv_done gate_act hid_tmp hid_high")
        (lora_loaded, lora_done, prep_step, near_ready, norm_step, ends_copied, sigw_ready, agate_ready, ggate_ready, ksq_ready, vs_ready,
         cum_ready, ksum_ready, knorm_ready, decay_ready, invdec_ready, adec_ready, bdec_ready,
         kdec_ready, rdec_ready, rkr_ready, rkrsum_ready, bonus_ready) = signals(
            "lora_loaded lora_done prep_step near_ready norm_step ends_copied sigw_ready agate_ready ggate_ready ksq_ready vs_ready cum_ready "
            "ksum_ready knorm_ready decay_ready invdec_ready adec_ready bdec_ready kdec_ready rdec_ready "
            "rkr_ready rkrsum_ready bonus_ready")
        (turned, natural, scored, masked, seed_ready, seed_turned, inv_first, off_ready, z_done,
         prod_ready, grown, inv_ready, invt_ready, x_done, x_ready2, wu_done, w_ready, u_ready, tr_done,
         tr_ready, rhat_done, rhat_ready, gain_done, gain_ready, carried, state_ready, y_done, y_ready,
         mean_done, dev_ready, devsq_ready, var_done, ystd_ready, tile_done, z_high, z_low) = signals(
            "turned natural scored masked seed_ready seed_turned inv_first off_ready z_done prod_ready grown "
            "inv_ready invt_ready x_done x_ready2 wu_done w_ready u_ready tr_done tr_ready rhat_done "
            "rhat_ready gain_done gain_ready carried state_ready y_done y_ready mean_done dev_ready "
            "devsq_ready var_done ystd_ready tile_done z_high z_low")
        (rope_term, rope_k, kv_ready, q_nope, q_rope, vtok_done, vtok_ready, s_done, max_ready, bias_ready,
         exp_done, pinv_ready, prob_ready, pt_done, pt_ready, o_done, o_high, o_low) = signals(
            "rope_term rope_k kv_ready q_nope q_rope vtok_done vtok_ready s_done max_ready bias_ready exp_done "
            "pinv_ready prob_ready pt_done pt_ready o_done o_high o_low")
        (pool_loaded, pool_win, pool_dev, pool_done, pool_tmp, pool_high, pool_low, v2_done, v2_ready,
         q2_copied, s2_done, s2_biased, max2, bias2_ready, sink2_done, den2, inv2, p2_ready, p2t_done,
         p2t_ready, o2_done, ya_high, ya_low, mix_b, merged_tmp, merged_high) = signals(
            "pool_loaded pool_win pool_dev pool_done pool_tmp pool_high pool_low v2_done v2_ready q2_copied "
            "s2_done s2_biased max2 bias2_ready sink2_done den2 inv2 p2_ready p2t_done p2t_ready o2_done "
            "ya_high ya_low mix_b merged_tmp merged_high")

        def fixed_wait(eng):
            eng.wait_ge(const_loaded, 32)

        def wait_evacuated(eng, name):
            for s in range(SLOTS):
                eng.wait_ge(bank_free[s], START[FOLLOWS[name]][s])

        def read_down(act, i, r, c, first=0):
            if first == 0 and r == 2:
                return
            act.wait_ge(unit_done[r], c + 1)
            act.activation(down[:, first + r, :], bank[r][:, :], ACT.Copy).then_inc(bank_free[r], 1)

        def pool_split(dve, g):
            dve.wait_ge(pool_high, g + 1)
            dve.tensor_tensor(yp[1][:, g, :], tmp[0][:, :], yp[0][:, g, :].bitcast(F32), ALU.subtract)\
                .then_inc(pool_low, 1)

        block = ctx.enter_context(nc.Block())

        @block.sync
        def _(sp):
            sp.dma_start(consts[:, :], dram["consts"]).then_inc(const_loaded, 16)
            sp.dma_start(vecs[:, :], dram["vecs"]).then_inc(const_loaded, 16)
            sp.dma_start(x[:, :, :], dram["x"]).then_inc(x_loaded, 16)

            def load(name):
                def body(i, r, c):
                    n = KS[name][r]
                    src = dram[f"{name}{r}"][bass.ds(i, 1)] if name in BY_SLOT else dram[name][bass.ds(SLOTS * i + r, 1)]
                    sp.wait_ge(w_split[r], c)
                    sp.dma_start(raw[r][:, 0:n, :], src.rearrange("a p k n -> p (a k) n")).then_inc(w_loaded[r], 16)
                over_units(sp, name, body)

            def load_ffn(tag):
                for p in range(len(PARTS)):
                    load(f"{tag}gu{p}")
                    load(f"{tag}dn{p}")

            for name in ("lora", "r", "k", "v"):
                load(name)
            def load_tile(j):
                sp.dma_start(lora2[:, :, :], dram["lora2"][bass.ds(j, 1)].rearrange("a p k n -> p (a k) n"))\
                    .then_inc(lora_loaded, 16)
                if not isinstance(j, int):
                    sp.wait_ge(bonus_ready, j)
                sp.dma_start(tvec[:, 0:len(TILE_VECS)], dram["tvec"][bass.ds(j, 1)].rearrange("a p n -> p (a n)"))\
                    .then_inc(lora_loaded, 16)
            load_tile(0)
            with sp.Fori(1, DT) as j:
                sp.wait_ge(lora_done, j * 3)
                load_tile(j)
            sp.wait_ge(tile_done, DT)
            sp.dma_start(x[:, :, :], dram["x"]).then_inc(x_back, 16)
            sp.dma_start(late[:, :], dram["late"]).then_inc(const_loaded, 16)
            load("w_o")
            load_ffn("f0")
            for name in ("kvd", "qd", "heads", "o_w"):
                load(name)
            load_ffn("f1")
            load("in")
            wait_evacuated(sp, "f1dn2")
            sp.dma_start(pool_w[:, :, :], dram["pool_w"]).then_inc(pool_loaded, 16)
            load("mix")
            load("out")
            load_ffn("f2")
            for j in range(DT):
                sp.wait_ge(out_ready, j + 1)
                sp.dma_start(out_d[:, j, :], x[:, j, :]).then_inc(out_stored, 16)
            sp.wait_ge(out_stored, 16 * DT)

        @block.gpsimd
        def _(pool):
            with pool.Fori(0, DT) as j:
                for lv in range(1, LEVELS + 1):
                    for p in range(2):
                        if lv == 1:
                            pool.wait_ge(masked, j * 8 + (SCORES.index((p, 0)) + 1))
                        else:
                            pool.wait_ge(z_done, j * 2 * LEVELS + 2 * (lv - 2) + p + 1)
                        mask = const("level", lo=lv * P, hi=(lv + 1) * P).unsqueeze(1).broadcast_to([P, TT, P])
                        pool.tensor_tensor(off[p][:, :, :], ab[p][:, :, :], mask, ALU.mult).then_inc(off_ready, 1)

        @block.scalar
        def _(act):
            def high(name, i, r, c):
                n = KS[name][r]
                act.wait_ge(w_loaded[r], (c + 1) * 16)
                act.wait_ge(unit_done[r], c)
                act.activation(w_hi[r][:, 0:n, :], raw[r][:, 0:n, :], ACT.Copy).then_inc(w_high[r], 1)

            def norm(name, source, ready):
                i, first, n = NORM_AT[name]
                for j in range(n):
                    ready(j)
                    if j >= 2:
                        act.wait_ge(sq_used, first - i + j - 1)
                    act.activation(sq[(first + j) % 2][:, :], source(j), ACT.Square).then_inc(sq_ready, 1)
                act.wait_ge(sum_ready, i + 1)
                if i:
                    act.wait_ge(rstd_ready, i)
                act.activation(std[:, :], bank[7][:, :], ACT.Sqrt, scale=1.0 / (n * P),
                               bias=const("eps")).then_inc(std_ready, 1)

            def normed(name, dst):
                first, n = NORMED_AT[name]
                for j in range(n):
                    act.wait_ge(normed_tmp, first + j + 1)
                    act.activation(dst[0][:, j, :], tmp[j % 2][:, :], ACT.Copy).then_inc(normed_high, 1)

            def x_updated(name):
                return lambda j: act.wait_ge(x_ready, RESID_AT[name] + j + 1)

            def mix_tile(phase, j, par):
                q, which, dst = MIXES[phase]
                act.activation(sq[par][:, :], tile(hp, j, 1, T + 1), ACT.Copy,
                               scale=column(omu, which * DT, j)).then_inc(mix_base, 1)
                act.wait_ge(mix_tmp, j + (q * DT + 1))
                act.activation(tile(opnd[dst][0], j), tmp[par][:, :], ACT.Copy).then_inc(mix_high, 1)

            def read_out(name, write, mix=None):
                def body(i, r, c):
                    act.wait_ge(unit_done[r], c + 1)
                    write(i, r).then_inc(bank_free[r], 1)
                    if mix is not None:
                        mix_tile(mix, SLOTS * i + r, r % 2)
                over_units(act, name, body, high)

            act.wait_ge(const_loaded, 32)
            norm("n_mix", lambda j: x[:, j, :], lambda j: act.wait_ge(x_loaded, 16))
            start_ahead(high, "lora")
            act.wait_ge(h_ready, DT + 1)
            act.wait_ge(omu_ready, 1)
            for phase in ("w1", "a1"):
                for j in range(DT):
                    mix_tile(phase, j, j % 2)

            def read_lora(i, r, c):
                act.wait_ge(unit_done[r], c + 1)
                rows = (slice(0, 64), slice(64, P), slice(0, P), slice(0, G_REST))[r]
                dst = (lora_wa, lora_wa, lora_g0, lora_g1)[r]
                act.activation(dst[rows, :], bank[r][rows, :], (ACT.Tanh, ACT.Copy, ACT.Sigmoid, ACT.Sigmoid)[r])\
                    .then_inc(bank_free[r], 1)
                if r < 2:
                    for j in range(DT):
                        mix_tile(("g1", "r")[r], j, j % 2)
            over_units(act, "lora", read_lora, high)
            read_out("r", lambda i, r: act.activation(tile(r_t, SLOTS * i + r), bank[r][:, :], ACT.Copy), "k")
            read_out("k", lambda i, r: act.activation(tile(k_t, SLOTS * i + r), bank[r][:, :], ACT.Copy), "v")
            read_out("v", lambda i, r: act.activation(tile(v_t, SLOTS * i + r), bank[r][:, :], ACT.Copy))

            def tv(name):
                n = TILE_VECS.index(name)
                return tvec[:, n:n + 1]

            def prep_inputs(q):
                act.wait_ge(lora_loaded, q * 32 + 32)
                act.activation(k_sq[:, :], tile(k_t, q), ACT.Square, scale=tv("k_k")).then_inc(ksq_ready, 1)
                act.activation(v_s[:, :], tile(v_t, q), ACT.Copy).then_inc(vs_ready, 1)

            def prep_norm(q):
                act.wait_ge(ksum_ready, q + 1)
                act.activation(k_norm[:, :], bank[7][:, :], ACT.Sqrt).then_inc(knorm_ready, 1)

            def prep_sigmoids(q):
                act.wait_ge(lora_done, q * 3 + 1)
                act.activation(sig_w[:, :], bank[3][:, :], ACT.Sigmoid, bias=tv("w0")).then_inc(sigw_ready, 1)
                act.wait_ge(lora_done, q * 3 + 2)
                act.activation(a_gate[:, :], bank[7][:, :], ACT.Sigmoid, bias=tv("a0")).then_inc(agate_ready, 1)

            def prep_decay(q, first=False):
                act.wait_ge(cum_ready, q + 1)
                if not first:
                    act.wait_ge(ends_copied, q)
                c3 = cum[:, :].rearrange("p (c t) -> p c t", c=NCH)
                act.activation(decay[:, :, 1:CHUNK + 1], c3, ACT.Exp, scale=-DECAY_C).then_inc(decay_ready, 1)
                act.activation(inv_decay[:, :], cum[:, :], ACT.Exp, scale=DECAY_C).then_inc(invdec_ready, 1)
                gate_there = act.to_reg(q * 3 + 3)
                fixed_wait(act)
                act.wait_ge(lora_done, gate_there)
                act.wait_ge(vs_ready, q + 1)
                act.activation(tile(v_t, q), bank[3][:, :], ACT.Copy).then_inc(ggate_ready, 1)

            def natural_copy(q, n):
                b, dst = ((0, a_nat), (1, b_nat), (2, k_nat), (3, v_nat))[n]
                act.wait_ge(turned, q * 4 + (n + 1))
                act.activation(dst[:, :, :], bank[b][:, :].rearrange("p (c n) -> p c n", c=TT), ACT.Copy)\
                    .then_inc(natural, 1)

            def seed_copies(q):
                for p in range(2):
                    act.wait_ge(seed_turned, q * 2 + (p + 1))
                    act.activation(inv[p][:, :, :], bank[4 - 4 * p][:, :].rearrange("p (c n) -> p c n", c=TT), ACT.Copy)\
                        .then_inc(inv_first, 1)

            def copy_output(j):
                act.wait_ge(y_done, j + 1)
                act.activation(y_t[:, :], bank[3][:, :], ACT.Copy).then_inc(y_ready, 1)

            def deviation(j):
                act.wait_ge(dev_ready, j + 1)
                act.activation(y_sq[:, :], y_dev[:, :], ACT.Square).then_inc(devsq_ready, 1)

            def deviation_root(j):
                act.wait_ge(var_done, j + 1)
                act.activation(y_std[:, :], bank[7][:, :], ACT.Sqrt, bias=const("lnx_eps")).then_inc(ystd_ready, 1)

            def core(j, ahead=True):
                for lv in range(1, LEVELS + 1):
                    for p in range(2):
                        act.wait_ge(z_done, j * 2 * LEVELS + (2 * (lv - 1) + p + 1))
                        act.activation(prod[p][:, :, :], bank[4 - 4 * p][:, :].rearrange("p (c n) -> p c n", c=TT),
                                       ACT.Copy).then_inc(prod_ready, 1)
                    if lv == 1:
                        act.wait_ge(x_done, j + 1)
                        act.activation(x_nat[:, :, :], bank[7][:, :].rearrange("p (c n) -> p c n", c=TT), ACT.Copy)\
                            .then_inc(x_ready2, 1)
                    if ahead:
                        if lv == 1:
                            if not isinstance(j, int):
                                act.wait_ge(tile_done, j)
                            prep_inputs(j + 1)
                        elif lv == 2:
                            prep_norm(j + 1)
                        elif lv == 3:
                            prep_sigmoids(j + 1)
                        elif lv == 4:
                            prep_decay(j + 1)
                act.wait_ge(wu_done, j * 2 + 1)
                act.activation(w_nat[:, :, :], bank[4][:, :].rearrange("p (c n) -> p c n", c=TT), ACT.Copy)\
                    .then_inc(w_ready, 1)
                copy_output(j)

            prep_inputs(0)
            prep_norm(0)
            prep_sigmoids(0)
            prep_decay(0, True)
            for n in range(4):
                natural_copy(0, n)
            seed_copies(0)
            with act.Fori(0, DT - 1) as j:
                core(j)
                natural_copy(j + 1, 0)
                natural_copy(j + 1, 1)
                natural_copy(j + 1, 2)
                deviation(j)
                natural_copy(j + 1, 3)
                deviation_root(j)
                seed_copies(j + 1)
            core(DT - 1, False)
            deviation(DT - 1)
            deviation_root(DT - 1)

            act.wait_ge(tile_done, DT)
            for j in range(DT):
                act.activation(opnd["a"][0][:, j, :], z_t[:, j, :], ACT.Copy).then_inc(z_high, 1)
            start_ahead(high, "w_o")
            read_out("w_o", lambda i, r: act.activation(tile(m, SLOTS * i + r), bank[r][:, :], ACT.Copy))
            norm("n_wo", lambda j: m[:, j, :], lambda j: wait_evacuated(act, "w_o") if j == 0 else None)
            norm("n_f0", lambda j: x[:, j, :], x_updated("w_o"))

            def ffn(tag):
                for p, kt in enumerate(PARTS):
                    hidden = HIDDEN_AT[tag] + sum(PARTS[:p])

                    def gate_up(i, r, c):
                        h = 2 * i + (hidden + r // 2)
                        if r % 2 == 0:
                            act.wait_ge(unit_done[r], c + 1)
                            if tag == "f2":
                                act.wait_ge(hid_tmp, h)
                                act.activation(gact[0][:, :], bank[r][:, :], ACT.Silu).then_inc(bank_free[r], 1)
                            else:
                                ft = 2 * i + (sum(PARTS[:p]) + r // 2)
                                base = VEC["conv"][0] + (0 if tag == "f0" else FT * 4)
                                act.wait_ge(conv_done, h)
                                act.activation(gpad[:, 2:T + 2], bank[r][:, :], ACT.Copy).then_inc(gate_padded, 1)
                                act.wait_ge(gate_act, h)
                                act.activation(gconv[:, :], bank[r][:, :], ACT.Identity,
                                               scale=column(vecs, base + 2, 4 * ft), bias=column(vecs, base + 3, 4 * ft))\
                                    .then_inc(bank_free[r], 1)
                        else:
                            if tag != "f2":
                                act.wait_ge(conv_done, h + 1)
                                act.wait_ge(hid_tmp, h)
                                act.activation(gact[0][:, :], gconv[:, :], ACT.Gelu_apprx_tanh).then_inc(gate_act, 1)
                            act.wait_ge(hid_tmp, h + 1)
                            act.activation(tile(opnd["b"][0], 2 * i + r // 2), tmp[(r // 2) % 2][:, :], ACT.Copy)\
                                .then_inc(hid_high, 1)
                    over_units(act, f"{tag}gu{p}", gate_up, high)
                    over_units(act, f"{tag}dn{p}", lambda i, r, c: None, high)

            normed("f0", opnd["a"])
            ffn("f0")
            norm("n_f0out", lambda j: m[:, j, :], lambda j: wait_evacuated(act, "f0dn2") if j == 0 else None)
            norm("n_mla", lambda j: x[:, j, :], x_updated("f0"))

            normed("kv", opnd["a"])
            normed("q", opnd["b"])
            over_units(act, "kvd", lambda i, r, c: read_down(act, i, r, c), high)
            norm("n_ckv", lambda j: down[:, j, :], lambda j: act.wait_ge(bank_free[j], START["kvd"][j] + 1))
            normed("ckv", ckv)
            over_units(act, "qd", lambda i, r, c: read_down(act, i, r, c, 2), high)
            norm("n_cq", lambda j: down[:, 2 + j, :], lambda j: act.wait_ge(bank_free[j], START["qd"][j] + 1))
            normed("cq", cq)

            def head(i, r, c):
                p = r // 2
                act.wait_ge(unit_done[r], c + 1)
                if r % 2 == 0:
                    act.activation(kf[p][0:NOPE, :], bank[r][0:NOPE, :], ACT.Copy).then_inc(kv_ready, 1)
                    act.activation(v_tr[p][NOPE:P, :], bank[r][NOPE:P, :], ACT.Copy).then_inc(bank_free[r], 1)
                else:
                    act.activation(qf[p][0:NOPE, :], bank[r][0:NOPE, :], ACT.Copy).then_inc(q_nope, 1)
                if r == SLOTS - 1:
                    attend(i)

            def attend(i):
                for p in range(2):
                    act.wait_ge(vtok_done, i * 2 + (p + 1))
                    act.activation(v_tok[p][:, :, :], bank[6 + p][:, 0:TT * HEAD].rearrange("p (c n) -> p c n", c=TT),
                                   ACT.Copy).then_inc(vtok_ready, 1)

                def exp(t):
                    n = (t // 2 + 1) * P
                    act.wait_ge(bias_ready, i * 8 + (t + 1))
                    act.activation(prob[t % 4][:, 0:n], bank[4 + t % 2][:, 0:n], ACT.Exp, scale=MLA_SCALE,
                                   bias=stat[:, 8 + t:9 + t], accum_out=stat[:, 16 + t:17 + t]).then_inc(exp_done, 1)

                exp(0)
                for t in range(8):
                    b, n = t // 2, t // 2 + 1
                    if t + 1 < 8:
                        exp(t + 1)
                    act.wait_ge(pt_done, i * 8 + (t + 1))
                    act.activation(prob_t[t % 2][:, 0:n, b * P:(b + 1) * P],
                                   bank[6][:, 0:n * P].rearrange("p (c n) -> p c n", c=n), ACT.Copy)\
                        .then_inc(pt_ready, 1)
                act.wait_ge(o_done, i + 1)
                act.activation(tile(opnd["a"][0], i), bank[7][:, :], ACT.Copy).then_inc(o_high, 1)

            over_units(act, "heads", head, high)
            read_out("o_w", lambda i, r: act.activation(tile(m, SLOTS * i + r), bank[r][:, :], ACT.Copy))
            norm("n_ow", lambda j: m[:, j, :], lambda j: wait_evacuated(act, "o_w") if j == 0 else None)
            norm("n_f1", lambda j: x[:, j, :], x_updated("o_w"))
            normed("f1", opnd["a"])
            ffn("f1")
            norm("n_f1out", lambda j: m[:, j, :], lambda j: wait_evacuated(act, "f1dn2") if j == 0 else None)
            norm("n_in", lambda j: x[:, j, :], x_updated("f1"))
            normed("in", opnd["a"])

            def read_in(i, r, c):
                u = SLOTS * i + r
                act.wait_ge(unit_done[r], c + 1)
                if u < 4:
                    act.activation(z2[:, u, PAD:PAD + T], bank[r][:, :], ACT.Copy).then_inc(bank_free[r], 1)
                elif u < 8:
                    act.activation(q2[:, u - 4, :], bank[r][:, :], ACT.Copy, scale=HEAD ** -0.5).then_inc(bank_free[r], 1)
                else:
                    act.activation((k2, v2)[u - 8][:, :], bank[r][:, :], ACT.Copy).then_inc(bank_free[r], 1)
            over_units(act, "in", read_in, high)

            for g in range(4):
                act.wait_ge(pool_done, g + 1)
                act.wait_ge(pool_low, g)
                act.activation(tmp[0][:, :], bank[4][:, :], ACT.Copy, scale=vec("pool_scale", g)).then_inc(pool_tmp, 1)
                act.wait_ge(pool_tmp, g + 1)
                act.activation(yp[0][:, g, :], tmp[0][:, :], ACT.Copy).then_inc(pool_high, 1)
            act.wait_ge(v2_done, 1)
            act.activation(v2n[:, :, :], bank[5][:, :].rearrange("p (c n) -> p c n", c=TT), ACT.Copy).then_inc(v2_ready, 1)
            wait_evacuated(act, "in")
            with act.Fori(0, 4) as j:
                act.wait_ge(ya_high, j)
                act.activation(q2s[:, :], tile(q2, j), ACT.Copy).then_inc(q2_copied, 1)
                for t in range(8):
                    p, n = t % 2, t // 2
                    lo, hi = max(n - 1, 0), min(n + 2, TT)
                    w = (hi - lo) * P
                    act.wait_ge(bias2_ready, j * 8 + (t + 1))
                    act.activation(s2[p][:, 0:w], s2[p][:, 0:w], ACT.Exp, bias=stat[:, 8 * p + 2:8 * p + 3],
                                   accum_out=stat[:, 8 * p + 3:8 * p + 4])
                    act.activation(stat[:, 8 * p + 4:8 * p + 5], column(vecs, VEC["sink"][0] + 4 * p, j), ACT.Exp,
                                   bias=stat[:, 8 * p + 2:8 * p + 3]).then_inc(sink2_done, 1)
                    act.wait_ge(p2t_done, j * 8 + (t + 1))
                    act.activation(p2t[p][:, 0:hi - lo, :], bank[6][:, 0:w].rearrange("p (c n) -> p c n", c=hi - lo),
                                   ACT.Copy).then_inc(p2t_ready, 1)
                act.wait_ge(o2_done, j + 1)
                act.activation(tile(ya[0], j), bank[7][:, :], ACT.Copy).then_inc(ya_high, 1)

            def mix(i, r, c):
                if r < 2:
                    act.wait_ge(unit_done[r], c + 1)
                    act.wait_ge(mix_b, i)
                    act.activation(gates[r][:, :], bank[r][:, :], ACT.Sigmoid).then_inc(bank_free[r], 1)
                if r == SLOTS - 1:
                    act.wait_ge(merged_tmp, i + 1)
                    act.activation(tile(opnd["c"][0], i), tmp[0][:, :], ACT.Copy).then_inc(merged_high, 1)
            over_units(act, "mix", mix, high)
            over_units(act, "out", lambda i, r, c: None, high)
            norm("n_f2", lambda j: x[:, j, :], lambda j: wait_evacuated(act, "out") if j == 0 else None)
            normed("f2", opnd["a"])
            ffn("f2")
            norm("n_final", lambda j: x[:, j, :], lambda j: wait_evacuated(act, "f2dn2") if j == 0 else None)

        @block.vector
        def _(dve):
            def low(name, i, r, c):
                n = KS[name][r]
                dve.wait_ge(w_high[r], c + 1)
                dve.wait_ge(unit_done[r], c)
                dve.tensor_tensor(w_lo[r][:, 0:n, :], raw[r][:, 0:n, :], w_hi[r][:, 0:n, :].bitcast(F32),
                                  ALU.subtract).then_inc(w_split[r], 1)

            def root(name):
                i = NORM_AT[name][0]
                dve.wait_ge(std_ready, i + 1)
                dve.reciprocal(rstd[:, :], std[:, :]).then_inc(rstd_ready, 1)
                dve.wait_ge(rstd_ready, i + 1)

            def residual(name, gain):
                for j in range(DT):
                    k = RESID_AT[name] + j
                    dve.scalar_tensor_tensor(tmp[j % 2][:, :], m[:, j, :], vec(gain[0], gain[1] + j), rstd[:, :],
                                             ALU.mult, ALU.mult).then_inc(resid_tmp, 1)
                    dve.wait_ge(resid_tmp, k + 1)
                    dve.tensor_tensor(x[:, j, :], x[:, j, :], tmp[j % 2][:, :], ALU.add).then_inc(x_ready, 1)
                dve.wait_ge(x_ready, RESID_AT[name] + DT)

            def normed(name, src, gain, dst):
                first, n = NORMED_AT[name]

                def scale(j):
                    dve.scalar_tensor_tensor(tmp[j % 2][:, :], src(j), vec(gain[0], gain[1] + j), rstd[:, :],
                                             ALU.mult, ALU.mult).then_inc(normed_tmp, 1)
                if first:
                    dve.wait_ge(normed_low, first)
                scale(0)
                for j in range(n):
                    if j + 1 < n:
                        if j >= 1:
                            dve.wait_ge(normed_low, first + j)
                        scale(j + 1)
                    dve.wait_ge(normed_high, first + j + 1)
                    dve.tensor_tensor(dst[1][:, j, :], tmp[j % 2][:, :], dst[0][:, j, :].bitcast(F32),
                                      ALU.subtract).then_inc(normed_low, 1)

            def mix_tile(phase, j, par):
                q, which, dst = MIXES[phase]
                dve.wait_ge(mix_base, j + (q * DT + 1))
                dve.scalar_tensor_tensor(tmp[par][:, :], tile(hp, j, 0, T), column(vecs, VEC["mu"][0] + which * DT, j),
                                         sq[par][:, :], ALU.mult, ALU.add).then_inc(mix_tmp, 1)
                dve.wait_ge(mix_high, j + (q * DT + 1))
                dve.tensor_tensor(tile(opnd[dst][1], j), tmp[par][:, :], tile(opnd[dst][0], j).bitcast(F32),
                                  ALU.subtract).then_inc(mix_low, 1)

            def mixing(name, mix):
                over_units(dve, name, lambda i, r, c: mix_tile(mix, SLOTS * i + r, r % 2), low)

            dve.memset(hp[:, :, 0:1], 0.0).then_inc(h_ready, 1)
            dve.memset(decay[:, :, 0:1], 1.0).then_inc(zeroed, 1)
            dve.wait_ge(const_loaded, 32)
            mu0 = VEC["mu"][0]
            dve.tensor_scalar(omu[:, :], vecs[:, mu0:mu0 + 48], -1.0, 1.0, ALU.mult, ALU.add).then_inc(omu_ready, 1)
            root("n_mix")
            for j in range(DT):
                dve.scalar_tensor_tensor(hp[:, j, 1:T + 1], x[:, j, :], vec("norm_g", j), rstd[:, :],
                                         ALU.mult, ALU.mult).then_inc(h_ready, 1)
            start_ahead(low, "lora")
            dve.wait_ge(h_ready, DT + 1)
            for phase in ("w1", "a1"):
                for j in range(DT):
                    mix_tile(phase, j, j % 2)

            def lora(i, r, c):
                if r < 2:
                    for j in range(DT):
                        mix_tile(("g1", "r")[r], j, j % 2)
            over_units(dve, "lora", lora, low)
            mixing("r", "k")
            mixing("k", "v")
            over_units(dve, "v", lambda i, r, c: None, low)

            def tv(name):
                n = TILE_VECS.index(name)
                return tvec[:, n:n + 1]

            omka = tvec[:, len(TILE_VECS):len(TILE_VECS) + 1]

            def chunks(buf):
                return buf[:, :].rearrange("p (c t) -> p c t", c=NCH)

            def halves(buf, h):
                return buf[:, h:NCH:2, :]

            def halves_of(b):
                return bank[b][:, 0:TT * HEAD].rearrange("p (c n) -> p c n", c=TT)

            def quads(b):
                return bank[b][:, :].rearrange("p (c n) -> p c n", c=TT)

            def each(name, lo=0, hi=None):
                return const(name, lo=lo, hi=hi).unsqueeze(1).broadcast_to([P, TT, P])

            def quarter(buf, n):
                return buf[:, n * P:(n + 1) * P]

            def prep_mix(q):
                dve.wait_ge(lora_loaded, q * 32 + 32)
                dve.tensor_scalar(omka, tv("k_a"), -1.0, 1.0, ALU.mult, ALU.add).then_inc(prep_step, 1)

            def prep_clamp(q):
                dve.wait_ge(knorm_ready, q + 1)
                dve.tensor_scalar(k_clamp[:, :], k_norm[:, :], 1e-12, None, ALU.max).then_inc(prep_step, 1)

            def prep_inverse(q, n):
                dve.wait_ge(prep_step, step(q, "kclamp"))
                dve.reciprocal(quarter(k_inv, n), quarter(k_clamp, n)).then_inc(prep_step, 1)

            def prep_cum(q):
                dve.wait_ge(sigw_ready, q + 1)
                dve.tensor_tensor_scan(cum[:, :], const("scan"), sig_w[:, :], 0.0, ALU.mult, ALU.add)\
                    .then_inc(cum_ready, 1)

            def prep_factor(q):
                dve.wait_ge(agate_ready, q + 1)
                dve.wait_ge(prep_step, step(q, "omka"))
                dve.tensor_scalar(k_fac[:, :], a_gate[:, :], tv("k_a"), omka, ALU.mult, ALU.add).then_inc(prep_step, 1)

            def prep_keys(q):
                dve.wait_ge(prep_step, step(q, "kfac"))
                dve.tensor_tensor(k_new[:, :], tile(k_t, q), k_fac[:, :], ALU.mult).then_inc(prep_step, 1)

            def prep_rkr(q):
                dve.wait_ge(prep_step, step(q, "knew"))
                dve.scalar_tensor_tensor(rkr[:, :], tile(r_t, q), tv("r_k"), k_new[:, :], ALU.mult, ALU.mult)\
                    .then_inc(rkr_ready, 1)

            def prep_normed(q):
                dve.wait_ge(prep_step, step(q, "kinv3"))
                dve.scalar_tensor_tensor(kk[:, :], tile(k_t, q), tv("k_k"), k_inv[:, :], ALU.mult, ALU.mult)\
                    .then_inc(prep_step, 1)

            def prep_rates(q):
                dve.wait_ge(prep_step, step(q, "kk"))
                dve.tensor_tensor(b_tok[:, :], kk[:, :], a_gate[:, :], ALU.mult).then_inc(prep_step, 1)

            def prep_a(q):
                dve.wait_ge(prep_step, step(q, "kk"))
                dve.wait_ge(decay_ready, q + 1)
                dve.scalar_tensor_tensor(chunks(a_dec), chunks(kk), -1.0, decay[:, :, 0:CHUNK], ALU.mult, ALU.mult)\
                    .then_inc(adec_ready, 1)

            def prep_b(q):
                dve.wait_ge(prep_step, step(q, "btok"))
                dve.wait_ge(invdec_ready, q + 1)
                dve.tensor_tensor(b_dec[:, :], b_tok[:, :], inv_decay[:, :], ALU.mult).then_inc(bdec_ready, 1)

            def prep_k(q):
                dve.wait_ge(invdec_ready, q + 1)
                dve.tensor_tensor(k_dec[:, :], k_new[:, :], inv_decay[:, :], ALU.mult).then_inc(kdec_ready, 1)

            def prep_r(q):
                dve.wait_ge(decay_ready, q + 1)
                dve.tensor_tensor(chunks(r_dec), tile(r_t, q).rearrange("p (c t) -> p c t", c=NCH),
                                  decay[:, :, 1:CHUNK + 1], ALU.mult).then_inc(rdec_ready, 1)

            def prep_bonus(q):
                dve.wait_ge(rkrsum_ready, q + 1)
                dve.wait_ge(vs_ready, q + 1)
                dve.wait_ge(prep_step, step(q, "kk"))
                dve.tensor_tensor(tile(k_t, q), bank[7][:, :], v_s[:, :], ALU.mult).then_inc(bonus_ready, 1)

            def masks(q):
                dve.wait_ge(decay_ready, q + 1)
                dve.tensor_copy(ends[:, :, :], decay[:, :, CHUNK:CHUNK + 1]).then_inc(ends_copied, 1)
                for i, (p, n) in enumerate(SCORES):
                    dst, mask = ((ab, "strict"), (rb, "incl"), (ak, "strict"), (rk, "incl"))[n]
                    dve.wait_ge(scored, q * 8 + (i + 1))
                    dve.tensor_tensor(dst[p][:, :, :], quads(4 - 4 * p + n), each(mask), ALU.mult).then_inc(masked, 1)
                    if n == 0:
                        dve.wait_ge(masked, q * 8 + (i + 1))
                        dve.tensor_tensor(prod[p][:, :, :], ab[p][:, :, :], each("level", 0, P), ALU.mult)\
                            .then_inc(near_ready, 1)
                        dve.wait_ge(near_ready, q * 2 + (p + 1))
                        dve.tensor_tensor(inv_t[p][:, :, :], prod[p][:, :, :], each("ident"), ALU.add)\
                            .then_inc(seed_ready, 1)

            def deviation(j):
                dve.wait_ge(y_ready, j + 1)
                dve.wait_ge(mean_done, j + 1)
                dve.tensor_tensor(y_dev[:, :], y_t[:, :], bank[7][:, :], ALU.subtract).then_inc(dev_ready, 1)

            def gated_output(j):
                dve.wait_ge(ystd_ready, j + 1)
                dve.reciprocal(y_rstd[:, :], y_std[:, :]).then_inc(norm_step, 1)
                dve.wait_ge(norm_step, j * 4 + 1)
                dve.tensor_tensor(y_n[:, :], y_dev[:, :], y_rstd[:, :], ALU.mult).then_inc(norm_step, 1)
                dve.wait_ge(norm_step, j * 4 + 2)
                dve.tensor_scalar(y_dev[:, :], y_n[:, :], vec("lnx_w", j), vec("lnx_b", j), ALU.mult, ALU.add)\
                    .then_inc(norm_step, 1)
                dve.wait_ge(norm_step, j * 4 + 3)
                dve.wait_ge(bonus_ready, j + 1)
                dve.tensor_tensor(y_n[:, :], y_dev[:, :], tile(k_t, j), ALU.add).then_inc(norm_step, 1)
                dve.wait_ge(norm_step, j * 4 + 4)
                dve.wait_ge(ggate_ready, j + 1)
                dve.tensor_tensor(tile(z_t, j), y_n[:, :], tile(v_t, j), ALU.mult).then_inc(tile_done, 1)

            def core(j, ahead=True):
                q = j + 1
                for lv in range(1, LEVELS + 1):
                    if ahead and lv == 4:
                        prep_cum(q)
                    for p in range(2):
                        b = 4 - 4 * p
                        if lv < LEVELS:
                            dve.wait_ge(grown, j * (4 * LEVELS - 2) + (4 * (lv - 1) + 2 * p + 1))
                            dve.tensor_tensor(inv[p][:, :, :], quads(b + 1), inv[p][:, :, :], ALU.add)\
                                .then_inc(inv_ready, 1)
                            dve.wait_ge(grown, j * (4 * LEVELS - 2) + (4 * (lv - 1) + 2 * p + 2))
                        else:
                            dve.wait_ge(grown, j * (4 * LEVELS - 2) + (4 * (lv - 1) + p + 1))
                        dve.tensor_tensor(inv_t[p][:, :, :], quads(b + 2), inv_t[p][:, :, :], ALU.add)\
                            .then_inc(invt_ready, 1)
                        if ahead and lv == 1 and p == 1:
                            prep_mix(q)
                        elif ahead and lv == 2 and p == 1:
                            prep_clamp(q)
                        elif ahead and lv == 3:
                            prep_inverse(q, 2 * p)
                            prep_inverse(q, 2 * p + 1)
                        elif ahead and lv == 4 and p == 0:
                            prep_factor(q)
                            prep_keys(q)
                        elif ahead and lv == 4:
                            prep_rkr(q)
                            prep_normed(q)
                if ahead:
                    prep_rates(q)
                    prep_a(q)
                    prep_b(q)
                dve.wait_ge(wu_done, j * 2 + 2)
                dve.tensor_copy(u_nat[:, :, :], quads(5)).then_inc(u_ready, 1)
                if ahead:
                    prep_bonus(q)
                dve.wait_ge(tr_done, j + 1)
                half = const("ident_half").unsqueeze(1).broadcast_to([P, TT, HEAD])
                for h in range(2):
                    dve.tensor_tensor(halves(chunks(trans), h), halves_of(1 - h), half, ALU.add).then_inc(tr_ready, 1)
                dve.wait_ge(rhat_done, j + 1)
                dve.tensor_tensor(r_hat[:, :], bank[2][:, :], r_dec[:, :], ALU.add).then_inc(rhat_ready, 1)
                if ahead:
                    prep_k(q)
                dve.wait_ge(gain_done, j + 1)
                dve.wait_ge(ends_copied, j + 1)
                for h in range(2):
                    dve.tensor_tensor(halves(gain, h), halves_of(6 + h),
                                      halves(ends, h)[:, :, 0:1].broadcast_to([P, TT, HEAD]), ALU.mult)\
                        .then_inc(gain_ready, 1)
                if ahead:
                    dve.wait_ge(rhat_ready, j + 1)
                    prep_r(q)
                dve.wait_ge(gain_ready, j * 2 + 2)
                for ch in range(1, NCH - 1):
                    dve.wait_ge(carried, j * (NCH - 2) + ch)
                    dve.scalar_tensor_tensor(states[:, ch + 1, :], bank[ch % 2][:, 0:HEAD], ends[:, ch, 0:1],
                                             gain[:, ch, :], ALU.mult, ALU.add).then_inc(state_ready, 1)
                deviation(j)

            prep_mix(0)
            prep_clamp(0)
            for n in range(4):
                prep_inverse(0, n)
            prep_cum(0)
            prep_factor(0)
            prep_keys(0)
            prep_normed(0)
            prep_rkr(0)
            prep_rates(0)
            prep_a(0)
            prep_b(0)
            prep_k(0)
            prep_bonus(0)
            prep_r(0)
            masks(0)
            with dve.Fori(0, DT - 1) as j:
                core(j)
                masks(j + 1)
                gated_output(j)
            core(DT - 1, False)
            gated_output(DT - 1)

            for j in range(DT):
                dve.wait_ge(z_high, j + 1)
                dve.tensor_tensor(opnd["a"][1][:, j, :], z_t[:, j, :], opnd["a"][0][:, j, :].bitcast(F32),
                                  ALU.subtract).then_inc(z_low, 1)
            start_ahead(low, "w_o")
            over_units(dve, "w_o", lambda i, r, c: None, low)
            root("n_wo")
            dve.wait_ge(x_back, 16)
            residual("w_o", ("norm_g", 8))
            root("n_f0")

            def ffn(tag):
                for p, kt in enumerate(PARTS):
                    hidden = HIDDEN_AT[tag] + sum(PARTS[:p])

                    def gate_up(i, r, c):
                        h = 2 * i + (hidden + r // 2)
                        if r % 2 == 0:
                            if tag == "f2":
                                return
                            ft = 2 * i + (sum(PARTS[:p]) + r // 2)
                            base = VEC["conv"][0] + (0 if tag == "f0" else FT * 4)
                            dve.wait_ge(gate_padded, h + 1)
                            dve.wait_ge(bank_free[r], c + 1)
                            dve.scalar_tensor_tensor(gconv[:, :], gpad[:, 1:T + 1], column(vecs, base + 1, 4 * ft),
                                                     gconv[:, :], ALU.mult, ALU.add).then_inc(conv0, 1)
                            dve.wait_ge(conv0, h + 1)
                            dve.scalar_tensor_tensor(gconv[:, :], gpad[:, 0:T], column(vecs, base, 4 * ft),
                                                     gconv[:, :], ALU.mult, ALU.add).then_inc(conv_done, 1)
                        else:
                            if tag == "f2":
                                dve.wait_ge(bank_free[r - 1], i + (START[f"{tag}gu{p}"][r - 1] + 1))
                            else:
                                dve.wait_ge(gate_act, h + 1)
                            dve.wait_ge(unit_done[r], c + 1)
                            par = (r // 2) % 2
                            dve.tensor_tensor(tmp[par][:, :], gact[0][:, :], bank[r][:, :], ALU.mult)\
                                .then_inc(hid_tmp, 1)
                            dve.wait_ge(hid_high, h + 1)
                            t = 2 * i + r // 2
                            dve.tensor_tensor(tile(opnd["b"][1], t), tmp[par][:, :], tile(opnd["b"][0], t).bitcast(F32),
                                              ALU.subtract).then_inc(bank_free[r], 1)

                    def read_down_proj(i, r, c):
                        t = SLOTS * i + r
                        dst = tile(x if tag == "f2" else m, t)
                        dve.wait_ge(unit_done[r], c + 1)
                        if p == 0 and tag != "f2":
                            dve.tensor_copy(dst, bank[r][:, :]).then_inc(bank_free[r], 1)
                        else:
                            ins = dve.tensor_tensor(dst, dst, bank[r][:, :], ALU.add)
                            ins.then_inc(bank_free[r], 1)
                    over_units(dve, f"{tag}gu{p}", gate_up, low)
                    if p:
                        wait_evacuated(dve, f"{tag}dn{p - 1}")
                    over_units(dve, f"{tag}dn{p}", read_down_proj, low)
                wait_evacuated(dve, f"{tag}dn{len(PARTS) - 1}")

            def x_tile(j):
                return x[:, j, :]

            normed("f0", x_tile, ("norm_g", 16), opnd["a"])
            dve.memset(gpad[:, 0:2], 0.0).then_inc(zeroed, 1)
            dve.wait_ge(zeroed, 2)
            ffn("f0")
            root("n_f0out")
            residual("f0", ("norm_g", 24))
            root("n_mla")

            dve.wait_ge(const_loaded, 48)
            normed("kv", x_tile, ("kv_norm", 0), opnd["a"])
            normed("q", x_tile, ("norm_g", 32), opnd["b"])

            rope_a, rope_b = gconv, gpad
            RK, RS = slice(NOPE, QK), slice(QK, P)

            def rotate(b):
                dve.tensor_tensor(rope_a[RK, :], b[RK, :], const("cossin", RK), ALU.mult).then_inc(rope_term, 1)
                return dve.tensor_tensor(rope_b[RK, 0:T], b[RS, :], const("cossin", RS), ALU.mult)

            def kvd(i, r, c):
                if r != 2:
                    return
                dve.wait_ge(unit_done[r], c + 1)
                rotate(bank[r]).then_inc(bank_free[r], 1)
                dve.wait_ge(rope_term, 1)
                dve.wait_ge(bank_free[r], c + 1)
                for p in range(2):
                    dve.tensor_tensor(kf[p][RK, :], rope_a[RK, :], rope_b[RK, 0:T], ALU.add).then_inc(rope_k, 1)
            over_units(dve, "kvd", kvd, low)
            root("n_ckv")
            normed("ckv", lambda j: down[:, j, :], ("kv_a_norm", 0), ckv)
            over_units(dve, "qd", lambda i, r, c: None, low)
            root("n_cq")
            normed("cq", lambda j: down[:, 2 + j, :], ("q_norm", 0), cq)

            def head(i, r, c):
                p = r // 2
                if r % 2 == 1:
                    k = 2 * i + (p + 1)
                    dve.wait_ge(q_nope, k)
                    dve.wait_ge(q_rope, k - 1)
                    rotate(bank[r]).then_inc(bank_free[r], 1)
                    dve.wait_ge(rope_term, k + 1)
                    dve.wait_ge(bank_free[r], c + 1)
                    dve.tensor_tensor(qf[p][RK, :], rope_a[RK, :], rope_b[RK, 0:T], ALU.add).then_inc(q_rope, 1)
                if r == SLOTS - 1:
                    attend(i)

            def attend(i):
                def maxima(t):
                    n = (t // 2 + 1) * P
                    dve.wait_ge(s_done, i * 8 + (t + 1))
                    dve.reduce_max(stat[:, t:t + 1], bank[4 + t % 2][:, 0:n], AX.X).then_inc(max_ready, 1)
                    dve.wait_ge(max_ready, i * 8 + (t + 1))
                    dve.tensor_scalar(stat[:, 8 + t:9 + t], stat[:, t:t + 1], -MLA_SCALE, None, ALU.mult)\
                        .then_inc(bias_ready, 1)

                maxima(0)
                maxima(1)
                for t in range(8):
                    n = (t // 2 + 1) * P
                    dve.wait_ge(exp_done, i * 8 + (t + 1))
                    dve.reciprocal(stat[:, 24 + t:25 + t], stat[:, 16 + t:17 + t]).then_inc(pinv_ready, 1)
                    dve.wait_ge(pinv_ready, i * 8 + (t + 1))
                    dve.tensor_scalar(prob[t % 4][:, 0:n], prob[t % 4][:, 0:n], stat[:, 24 + t:25 + t], None, ALU.mult)\
                        .then_inc(prob_ready, 1)
                    if t + 2 < 8:
                        maxima(t + 2)
                dve.wait_ge(o_high, i + 1)
                dve.tensor_tensor(tile(opnd["a"][1], i), bank[7][:, :], tile(opnd["a"][0], i).bitcast(F32),
                                  ALU.subtract).then_inc(o_low, 1)

            dve.wait_ge(rope_k, 2)
            over_units(dve, "heads", head, low)
            over_units(dve, "o_w", lambda i, r, c: None, low)
            root("n_ow")
            residual("o_w", ("norm_g", 40))
            root("n_f1")
            normed("f1", x_tile, ("norm_g", 48), opnd["a"])
            dve.memset(gpad[:, 0:2], 0.0).then_inc(zeroed, 1)
            dve.wait_ge(zeroed, 3)
            ffn("f1")
            root("n_f1out")
            residual("f1", ("norm_g", 56))
            root("n_in")
            normed("in", x_tile, ("norm_mix", 0), opnd["a"])
            dve.memset(z2[:, :, 0:PAD], 0.0).then_inc(zeroed, 1)
            dve.memset(z2[:, :, PAD + T:ZW], 0.0).then_inc(zeroed, 1)
            over_units(dve, "in", lambda i, r, c: None, low)

            wait_evacuated(dve, "in")
            dve.wait_ge(zeroed, 5)
            wins = 0
            for g, w in enumerate(POOL_W):
                src, length = z2[:, g, :], ZW
                k = 1
                while k < w:
                    dst = win[(wins + 0) % 2]
                    dve.tensor_tensor(dst[:, 0:length - k], src[:, 0:length - k], src[:, k:length], ALU.add)\
                        .then_inc(pool_win, 1)
                    wins += 1
                    dve.wait_ge(pool_win, wins)
                    src, length, k = dst, length - k, 2 * k
                o = PAD - w // 2
                if g:
                    dve.wait_ge(pool_done, g)
                dve.tensor_scalar(dev2[:, :], src[:, o:o + T], 1.0 / w, None, ALU.mult).then_inc(pool_win, 1)
                wins += 1
                dve.wait_ge(pool_win, wins)
                for e, lo in enumerate((0, T - PAD)):
                    a = (2 * g + e) * PAD
                    dve.tensor_tensor(dev2[:, lo:lo + PAD], src[:, o + lo:o + lo + PAD],
                                      const("inv_count", lo=a, hi=a + PAD), ALU.mult).then_inc(pool_win, 1)
                wins += 2
                dve.wait_ge(pool_win, wins)
                dve.tensor_tensor(dev2[:, :], dev2[:, :], z2[:, g, PAD:PAD + T], ALU.subtract).then_inc(pool_dev, 1)
                if g:
                    pool_split(dve, g - 1)
            pool_split(dve, 3)

            with dve.Fori(0, 4) as j:
                for t in range(8):
                    p, n = t % 2, t // 2
                    lo, hi = max(n - 1, 0), min(n + 2, TT)
                    w, off0 = (hi - lo) * P, (lo - n + 1) * P
                    o = 8 * p
                    if t >= 2:
                        dve.wait_ge(p2t_done, j * 8 + (t - 1))
                    dve.wait_ge(s2_done, j * 8 + (t + 1))
                    dve.scalar_tensor_tensor(s2[p][:, 0:w], const("absdist", lo=off0, hi=off0 + w),
                                             column(consts, CONST["slope"][0] + 4 * p, j), bank[4 + p][:, 0:w],
                                             ALU.mult, ALU.add).then_inc(s2_biased, 1)
                    dve.wait_ge(s2_biased, j * 8 + (t + 1))
                    dve.reduce_max(stat[:, o:o + 1], s2[p][:, 0:w], AX.X).then_inc(max2, 1)
                    dve.wait_ge(max2, j * 8 + (t + 1))
                    dve.tensor_scalar(stat[:, o + 2:o + 3], stat[:, o:o + 1], column(vecs, VEC["sink"][0] + 4 * p, j),
                                      -1.0, ALU.max, ALU.mult).then_inc(bias2_ready, 1)
                    dve.wait_ge(sink2_done, j * 8 + (t + 1))
                    dve.tensor_tensor(stat[:, o + 5:o + 6], stat[:, o + 3:o + 4], stat[:, o + 4:o + 5], ALU.add)\
                        .then_inc(den2, 1)
                    dve.wait_ge(den2, j * 8 + (t + 1))
                    dve.reciprocal(stat[:, o + 6:o + 7], stat[:, o + 5:o + 6]).then_inc(inv2, 1)
                    dve.wait_ge(inv2, j * 8 + (t + 1))
                    dve.tensor_scalar(s2[p][:, 0:w], s2[p][:, 0:w], stat[:, o + 6:o + 7], None, ALU.mult)\
                        .then_inc(p2_ready, 1)
                dve.wait_ge(ya_high, j + 1)
                dve.tensor_tensor(tile(ya[1], j), bank[7][:, :], tile(ya[0], j).bitcast(F32), ALU.subtract)\
                    .then_inc(ya_low, 1)

            def mix(i, r, c):
                if r >= 2:
                    dve.wait_ge(unit_done[r], c + 1)
                    dve.wait_ge(bank_free[r - 2], i + (START["mix"][r - 2] + 1))
                    dve.tensor_tensor(gates[r][:, :], gates[r - 2][:, :], bank[r][:, :], ALU.mult)\
                        .then_inc(bank_free[r], 1)
                if r == SLOTS - 1:
                    for s in (2, 3):
                        dve.wait_ge(bank_free[s], i + (START["mix"][s] + 1))
                    dve.tensor_tensor(tmp[0][:, :], gates[2][:, :], gates[3][:, :], ALU.add).then_inc(merged_tmp, 1)
                    dve.wait_ge(merged_high, i + 1)
                    dve.tensor_tensor(tile(opnd["c"][1], i), tmp[0][:, :], tile(opnd["c"][0], i).bitcast(F32),
                                      ALU.subtract).then_inc(mix_b, 1)
            over_units(dve, "mix", mix, low)

            def add_out(i, r, c):
                t = SLOTS * i + r
                dve.wait_ge(unit_done[r], c + 1)
                dve.tensor_tensor(tile(x, t), tile(x, t), bank[r][:, :], ALU.add).then_inc(bank_free[r], 1)
            over_units(dve, "out", add_out, low)
            root("n_f2")
            wait_evacuated(dve, "out")
            normed("f2", x_tile, ("norm_ffn", 0), opnd["a"])
            ffn("f2")
            root("n_final")
            for j in range(DT):
                dve.scalar_tensor_tensor(x[:, j, :], x[:, j, :], vec("norm_final", j), rstd[:, :],
                                         ALU.mult, ALU.mult).then_inc(out_ready, 1)

        @block.tensor
        def _(pe):
            def dense(name, operand, ready=None, then=None):
                def body(i, r, c):
                    hi, lo = operand(r)
                    kt = KS[name][r]
                    pe.wait_ge(w_split[r], c + 1)
                    pe.wait_ge(bank_free[r], c)
                    for k in range(kt):
                        if ready is not None and (r == 0 or name == "lora"):
                            ready(r, k)
                        for n, (w, a) in enumerate(((w_hi, hi), (w_lo, hi), (w_hi, lo))):
                            mm = pe.matmul(bank[r][:, :], w[r][:, k, :], a[:, k, :],
                                           start=(k == 0 and n == 0), stop=(k == kt - 1 and n == 2))
                    mm.then_inc(unit_done[r], 1)
                    if then is not None:
                        then(i, r)
                over_units(pe, name, body)

            def norm(name):
                i, first, n = NORM_AT[name]
                if i:
                    pe.wait_ge(std_ready, i)
                for j in range(n):
                    pe.wait_ge(sq_ready, first + j + 1)
                    mm = pe.matmul(bank[7][:, :], const("ones"), sq[(first + j) % 2][:, :], start=(j == 0),
                                   stop=(j == n - 1))
                    mm.then_inc(sum_ready if j == n - 1 else sq_used, 1)

            def normed(name):
                return lambda r, k: pe.wait_ge(normed_low, NORMED_AT[name][0] + k + 1)

            pe.wait_ge(const_loaded, 32)
            norm("n_mix")
            dense("lora", lambda r: opnd["aba"[min(r, 2)]], lambda r, k: pe.wait_ge(mix_low, min(r, 2) * DT + k + 1))
            for phase in ("r", "k", "v"):
                q, _, src = MIXES[phase]
                dense(phase, lambda r: opnd[src], lambda r, k: pe.wait_ge(mix_low, q * DT + k + 1))
            wait_evacuated(pe, "v")

            HP = [slice(0, HEAD), slice(HEAD, P)]

            def cols(c, n=P):
                return slice(c * n, (c + 1) * n)

            def key_norms(q):
                pe.wait_ge(ksq_ready, q + 1)
                pe.matmul(bank[7][:, :], const("head_ones"), k_sq[:, :], start=True, stop=True).then_inc(ksum_ready, 1)

            def decay_product(q):
                pe.wait_ge(lora_loaded, q * 32 + 32)
                pe.matmul(bank[3][:, :], lora2[0:64, 0, :], lora_wa[0:64, :], start=True, stop=True).then_inc(lora_done, 1)

            def rate_product(q):
                pe.wait_ge(knorm_ready, q + 1)
                pe.matmul(bank[7][:, :], lora2[64:P, 0, :], lora_wa[64:P, :], start=True, stop=True).then_inc(lora_done, 1)

            def gate_product(q):
                pe.wait_ge(sigw_ready, q + 1)
                pe.matmul(bank[3][:, :], lora2[:, 1, :], lora_g0[:, :], start=True, stop=False)
                pe.matmul(bank[3][:, :], lora2[0:G_REST, 2, :], lora_g1[:, :], start=False, stop=True)\
                    .then_inc(lora_done, 1)

            def bonus_sums(q):
                pe.wait_ge(agate_ready, q + 1)
                pe.wait_ge(rkr_ready, q + 1)
                pe.matmul(bank[7][:, :], const("head_ones"), rkr[:, :], start=True, stop=True).then_inc(rkrsum_ready, 1)

            def turn(b, src):
                for c in range(TT):
                    mm = pe.transpose(bank[b][:, cols(c)], src[:, cols(c)], const("ident"))
                mm.then_inc(turned, 1)

            def front(q, last=None):
                for b, signal, src in ((0, adec_ready, a_dec), (1, bdec_ready, b_dec), (2, kdec_ready, k_dec)):
                    pe.wait_ge(signal, q + 1)
                    turn(b, src)
                pe.wait_ge(vs_ready, q + 1)
                pe.wait_ge(bonus_ready, q + 1)
                if last is not None:
                    mean_of(last)
                pe.wait_ge(ggate_ready, q + 1)
                turn(3, v_s)
                pe.wait_ge(rdec_ready, q + 1)
                for p, n in SCORES:
                    left, right = ((b_dec, a_dec), (b_dec, r_dec), (k_dec, a_dec), (k_dec, r_dec))[n]
                    if (p, n) == (1, 0):
                        if last is not None:
                            variance_of(last)
                        pe.wait_ge(natural, q * 4 + 4)
                    if last is not None and (p, n) == (0, 3):
                        pe.wait_ge(ystd_ready, last + 1)
                    for c in range(TT):
                        mm = pe.matmul(bank[4 - 4 * p + n][:, cols(c)], left[HP[p], cols(c)], right[HP[p], cols(c)],
                                       start=True, stop=True)
                    mm.then_inc(scored, 1)
                for p in range(2):
                    pe.wait_ge(seed_ready, q * 2 + (p + 1))
                    for c in range(TT):
                        mm = pe.transpose(bank[4 - 4 * p][:, cols(c)], inv_t[p][:, c, :], const("ident"))
                    mm.then_inc(seed_turned, 1)

            def mean_of(j):
                pe.wait_ge(y_ready, j + 1)
                pe.matmul(bank[7][:, :], const("head_mean"), y_t[:, :], start=True, stop=True).then_inc(mean_done, 1)

            def variance_of(j):
                pe.wait_ge(devsq_ready, j + 1)
                pe.matmul(bank[7][:, :], const("head_mean"), y_sq[:, :], start=True, stop=True).then_inc(var_done, 1)

            def core(j, ahead=True):
                q = j + 1
                for lv in range(1, LEVELS + 1):
                    for p in range(2):
                        b = 4 - 4 * p
                        pe.wait_ge(off_ready, j * 2 * LEVELS + (2 * (lv - 1) + p + 1))
                        if lv == 1:
                            pe.wait_ge(inv_first, j * 2 + (p + 1))
                        else:
                            pe.wait_ge(inv_ready, j * 2 * (LEVELS - 1) + (2 * (lv - 2) + p + 1))
                        for c in range(TT):
                            mm = pe.matmul(bank[b][:, cols(c)], off[p][:, c, :], inv[p][:, c, :], start=True, stop=True)
                        mm.then_inc(z_done, 1)
                    if lv == 1:
                        pe.wait_ge(masked, j * 8 + 8)
                        for c in range(TT):
                            for p in range(2):
                                mm = pe.matmul(bank[7][:, c * P + p * HEAD:c * P + (p + 1) * HEAD], ak[p][:, c, :],
                                               v_nat[:, c, HP[p]], start=True, stop=True)
                        mm.then_inc(x_done, 1)
                    for p in range(2):
                        b = 4 - 4 * p
                        pe.wait_ge(prod_ready, j * 2 * LEVELS + (2 * (lv - 1) + p + 1))
                        if lv > 1:
                            pe.wait_ge(invt_ready, j * 2 * LEVELS + (2 * (lv - 2) + p + 1))
                        if lv < LEVELS:
                            for c in range(TT):
                                mm = pe.matmul(bank[b + 1][:, cols(c)], inv_t[p][:, c, :], prod[p][:, c, :],
                                               start=True, stop=True)
                            mm.then_inc(grown, 1)
                        for c in range(TT):
                            mm = pe.matmul(bank[b + 2][:, cols(c)], prod[p][:, c, :], inv_t[p][:, c, :],
                                           start=True, stop=True)
                        mm.then_inc(grown, 1)
                    if ahead and lv == 1:
                        pe.wait_ge(x_ready2, j + 1)
                        key_norms(q)
                        decay_product(q)
                    elif ahead and lv == 2:
                        rate_product(q)
                    elif ahead and lv == 3:
                        gate_product(q)
                    elif ahead and lv == 5:
                        bonus_sums(q)
                pe.wait_ge(invt_ready, j * 2 * LEVELS + 2 * LEVELS)
                pe.wait_ge(x_ready2, j + 1)
                for b, src in ((4, a_nat), (5, x_nat)):
                    for c in range(TT):
                        for p in range(2):
                            mm = pe.matmul(bank[b][:, c * P + p * HEAD:c * P + (p + 1) * HEAD], inv_t[p][:, c, :],
                                           src[:, c, HP[p]], start=True, stop=True)
                    mm.then_inc(wu_done, 1)
                fixed_wait(pe)
                pe.wait_ge(w_ready, j + 1)
                for h in range(2):
                    for c in range(TT):
                        for p in range(2):
                            mm = pe.matmul(bank[1 - h][HP[p], cols(c, HEAD)], w_nat[HP[h], c, HP[p]],
                                           b_nat[HP[h], c, HP[p]], start=True, stop=True)
                mm.then_inc(tr_done, 1)
                for c in range(TT):
                    for p in range(2):
                        mm = pe.matmul(bank[2][HP[p], cols(c)], w_nat[:, c, HP[p]], rb[p][:, c, :], start=True, stop=True)
                mm.then_inc(rhat_done, 1)
                fixed_wait(pe)
                pe.wait_ge(u_ready, j + 1)
                if ahead:
                    pe.wait_ge(bonus_ready, q + 1)
                for h in range(2):
                    for c in range(TT):
                        for p in range(2):
                            dst = bank[6 + h][HP[p], cols(c, HEAD)]
                            pe.matmul(dst, b_nat[HP[h], c, HP[p]], u_nat[HP[h], c, HP[p]], start=True, stop=False,
                                      skip_group_check=True)
                            mm = pe.matmul(dst, k_nat[HP[h], c, HP[p]], v_nat[HP[h], c, HP[p]], start=False, stop=True,
                                           skip_group_check=True)
                mm.then_inc(gain_done, 1)
                if ahead:
                    pe.wait_ge(ggate_ready, q + 1)
                for p in range(2):
                    for c in range(TT):
                        pe.matmul(bank[3][HP[p], cols(c)], u_nat[:, c, HP[p]], rb[p][:, c, :], start=(c == 0),
                                  stop=False, skip_group_check=True)
                    for c in range(TT):
                        pe.matmul(bank[3][HP[p], cols(c)], v_nat[:, c, HP[p]], rk[p][:, c, :], start=False,
                                  stop=False, skip_group_check=True)
                fixed_wait(pe)
                pe.wait_ge(tr_ready, j * 2 + 2)
                pe.wait_ge(rhat_ready, j + 1)
                pe.wait_ge(gain_ready, j * 2 + 2)
                for ch in range(1, NCH):
                    if ch > 1:
                        before_chunk = pe.to_reg(j * (NCH - 2) + (ch - 1)) if ahead else (NCH - 2) * j + ch - 1
                        fixed_wait(pe)
                        pe.wait_ge(state_ready, before_chunk)
                    before = gain if ch == 1 else states
                    at_ch = 0 if ch == 1 else ch
                    if ch < NCH - 1:
                        for p in range(2):
                            mm = pe.matmul(bank[ch % 2][HP[p], 0:HEAD], trans[HP[p], cols(ch, HEAD)],
                                           before[HP[p], at_ch, :], start=True, stop=True)
                        mm.then_inc(carried, 1)
                    for p in range(2):
                        mm = pe.matmul(bank[3][HP[p], cols(ch, CHUNK)], before[HP[p], at_ch, :],
                                       r_hat[HP[p], cols(ch, CHUNK)], start=False, stop=(ch == NCH - 1),
                                       skip_group_check=True)
                mm.then_inc(y_done, 1)

            key_norms(0)
            decay_product(0)
            rate_product(0)
            gate_product(0)
            bonus_sums(0)
            front(0)
            with pe.Fori(0, DT - 1) as j:
                core(j)
                front(j + 1, j)
            core(DT - 1, False)
            mean_of(DT - 1)
            variance_of(DT - 1)

            pe.wait_ge(tile_done, DT)
            dense("w_o", lambda r: opnd["a"], lambda r, k: pe.wait_ge(z_low, k + 1))
            norm("n_wo")
            norm("n_f0")

            def ffn(tag):
                for p, kt in enumerate(PARTS):
                    hidden = HIDDEN_AT[tag] + sum(PARTS[:p])
                    dense(f"{tag}gu{p}", lambda r: opnd["a"], normed(tag))

                    def hidden_low(r, k):
                        s = 1 + 2 * (k % 2)
                        pe.wait_ge(bank_free[s], START[f"{tag}gu{p}"][s] + k // 2 + 1)
                    dense(f"{tag}dn{p}", lambda r: opnd["b"], hidden_low)

            ffn("f0")
            norm("n_f0out")
            norm("n_mla")
            dense("kvd", lambda r: opnd["a"], normed("kv"))
            norm("n_ckv")
            dense("qd", lambda r: opnd["b"], normed("q"))
            norm("n_cq")

            def attend(i, r):
                if r != SLOTS - 1:
                    return
                for p in range(2):
                    fixed_wait(pe)
                    pe.wait_ge(bank_free[2 * p], i + (START["heads"][2 * p] + 1))
                    if p:
                        pe.wait_ge(o_low, i)
                    for c in range(TT):
                        mm = pe.transpose(bank[6 + p][:, cols(c, HEAD)], v_tr[p][NOPE:P, cols(c)],
                                          const("ident", slice(NOPE, P), NOPE, P))
                    mm.then_inc(vtok_done, 1)

                def scores(t):
                    p, b = t % 2, t // 2
                    n = (b + 1) * P
                    if t < 2:
                        pe.wait_ge(q_rope, i * 2 + (p + 1))
                        pe.wait_ge(kv_ready, i * 2 + (p + 1))
                    else:
                        pe.wait_ge(exp_done, i * 8 + (t - 1))
                    pe.matmul(bank[4 + p][:, 0:n], qf[p][0:QK, cols(b)], kf[p][0:QK, 0:n], start=True, stop=False,
                              skip_group_check=True)
                    pe.matmul(bank[4 + p][:, cols(b)], const("mask_q", slice(0, 1)), const("mask_k", slice(0, 1)),
                              start=False, stop=True, skip_group_check=True).then_inc(s_done, 1)

                scores(0)
                scores(1)
                for t in range(8):
                    if t + 2 < 8:
                        scores(t + 2)
                    if t == 0:
                        pe.wait_ge(vtok_ready, i * 2 + 1)
                    else:
                        pe.wait_ge(pt_ready, i * 8 + t)
                    pe.wait_ge(prob_ready, i * 8 + (t + 1))
                    for c in range(t // 2 + 1):
                        mm = pe.transpose(bank[6][:, cols(c)], prob[t % 4][:, cols(c)], const("ident"))
                    mm.then_inc(pt_done, 1)
                pe.wait_ge(vtok_ready, i * 2 + 2)
                for p in range(2):
                    pe.wait_ge(pt_ready, i * 8 + (7 + p))
                    for c in range(TT):
                        mm = pe.matmul(bank[7][HP[p], c * P:T], v_tok[p][:, c, :], prob_t[p][:, c, c * P:T],
                                       start=(c == 0), stop=(c == TT - 1), skip_group_check=True)
                mm.then_inc(o_done, 1)

            pe.wait_ge(rope_k, 2)
            pe.wait_ge(const_loaded, 48)

            pe.wait_ge(normed_low, NORMED_AT["cq"][0] + 3)
            dense("heads", lambda r: cq if r % 2 else ckv, None, attend)
            dense("o_w", lambda r: opnd["a"], lambda r, k: pe.wait_ge(o_low, k + 1))
            norm("n_ow")
            norm("n_f1")
            ffn("f1")
            norm("n_f1out")
            norm("n_in")
            dense("in", lambda r: opnd["a"], normed("in"))
            pe.wait_ge(pool_loaded, 16)
            wait_evacuated(pe, "in")
            for c in range(TT):
                mm = pe.transpose(bank[5][:, cols(c)], v2[:, cols(c)], const("ident"))
            mm.then_inc(v2_done, 1)
            for g in range(4):
                pe.wait_ge(pool_dev, g + 1)
                if g:
                    pe.wait_ge(pool_tmp, g)
                pe.matmul(bank[4][:, :], pool_w[:, g, :], dev2[:, :], start=True, stop=True).then_inc(pool_done, 1)
            pe.wait_ge(pool_tmp, 4)
            pe.wait_ge(v2_ready, 1)
            with pe.Fori(0, 4) as j:
                pe.wait_ge(q2_copied, j + 1)
                pe.wait_ge(ya_low, j)

                def scores2(t):
                    p, n = t % 2, t // 2
                    lo, hi = max(n - 1, 0), min(n + 2, TT)
                    if t >= 2:
                        pe.wait_ge(s2_biased, j * 8 + (t - 1))
                    pe.matmul(bank[4 + p][:, 0:(hi - lo) * P], q2s[HP[p], cols(n)], k2[HP[p], lo * P:hi * P],
                              start=True, stop=True).then_inc(s2_done, 1)

                scores2(0)
                for t in range(8):
                    p, n = t % 2, t // 2
                    lo, hi = max(n - 1, 0), min(n + 2, TT)
                    if t + 1 < 8:
                        scores2(t + 1)
                    pe.wait_ge(p2_ready, j * 8 + (t + 1))
                    if t:
                        pe.wait_ge(p2t_ready, j * 8 + t)
                    for c in range(hi - lo):
                        mm = pe.transpose(bank[6][:, cols(c)], s2[p][:, cols(c)], const("ident"))
                    mm.then_inc(p2t_done, 1)
                    pe.wait_ge(p2t_ready, j * 8 + (t + 1))
                    for c in range(hi - lo):
                        mm = pe.matmul(bank[7][HP[p], cols(n)], v2n[:, lo + c, HP[p]], p2t[p][:, c, :],
                                       start=(c == 0), stop=(c == hi - lo - 1), skip_group_check=True)
                mm.then_inc(o2_done, 1)

            pe.wait_ge(ya_low, 4)
            pe.wait_ge(pool_low, 4)
            dense("mix", lambda r: (opnd["a"], opnd["a"], yp, ya)[r])
            dense("out", lambda r: opnd["c"], lambda r, k: pe.wait_ge(mix_b, k + 1))
            norm("n_f2")
            ffn("f2")
            norm("n_final")


def constants():
    out = {"consts": np.zeros((P, NCONST), np.float32), "late": np.zeros((P, NLATE), np.float32)}

    def put(name, value):
        a, n = CONST[name] if name in CONST else LATE[name]
        out["consts" if name in CONST else "late"][:, a:a + n] = np.asarray(value, np.float64).reshape(-1, n)

    i = np.arange(P)
    s, t = i[:, None], i[None, :]
    put("eps", NORM_EPS)
    put("lnx_eps", LNX_EPS)
    put("slope", -(2.0 ** -np.arange(1.0, 9.0))[None])
    put("ones", np.ones((P, P)))
    same_head = s // HEAD == t // HEAD
    put("head_ones", same_head)
    put("head_mean", same_head / HEAD)
    put("ident", np.eye(P))
    put("ident_half", np.tile(np.eye(HEAD), (2, 1)))
    put("strict", same_head & (s < t))
    put("incl", same_head & (s <= t))
    level = [(s // (2 * b) == t // (2 * b)) & (s // b % 2 == 0) & (t // b % 2 == 1) for b in 2 ** np.arange(LEVELS + 1)]
    put("level", np.concatenate(level, 1))
    put("scan", (np.arange(T) % CHUNK != 0)[None])
    ang = np.arange(T)[None, :] * (1.0 / 10000.0 ** (np.arange(0, ROPE, 2) / ROPE))[:, None]
    cossin = np.zeros((P, T))
    cossin[NOPE:QK] = np.tile(np.cos(ang), (2, 1))
    cossin[QK:] = np.concatenate([-np.sin(ang), np.sin(ang)])
    put("cossin", cossin)
    dist = np.abs(i[:, None] - np.arange(3 * P)[None, :] + P).astype(np.float64)
    put("absdist", np.where(dist <= P, dist, 1e30))
    count = []
    for w in POOL_W:
        pos = np.arange(T)
        n = np.clip(pos + w // 2, 0, T) - np.clip(pos - w // 2, 0, T)
        count += [n[:PAD], n[T - PAD:]]
    put("inv_count", 1.0 / np.concatenate(count)[None])
    put("mask_q", (i < CHUNK)[None])
    put("mask_k", np.where(i >= CHUNK, NEG, 0.0)[None])
    return out


def units_of(w):
    k, n = w.shape
    return w.reshape(k // P, P, n // P, P).transpose(2, 1, 0, 3)


def pad_columns(w, lo, n):
    out = np.zeros((w.shape[0], n), w.dtype)
    out[:, lo:lo + w.shape[1]] = w
    return out


def lay_out(v):
    def per_tile(a):
        return a.reshape(-1, P).T

    out = {**constants(), "x": v["x"][0].T.reshape(DT, P, T).transpose(1, 0, 2)}
    conv = np.concatenate([v["ffn_conv_w"], v["ffn_conv_b"][:, None]], 1)
    out["vecs"] = np.concatenate([
        per_tile(v["norm_g"]), per_tile(v["a_mu"][0]), per_tile(v["kv_norm_g"]), per_tile(v["kv_a_norm_g"]),
        per_tile(v["q_norm_g"]), per_tile(v["norm_mix_2"]), per_tile(v["norm_ffn_2"]), per_tile(v["norm_final_2"]),
        per_tile(v["pool_scale_2"]), np.broadcast_to(v["sink_2"], (P, 8)),
        per_tile(v["a_lnx_w"]), per_tile(v["a_lnx_b"]),
        conv.reshape(2, 4, FT, P).transpose(3, 0, 2, 1).reshape(P, -1)], 1)
    g1 = v["a_g1"][0]
    out["lora"] = np.concatenate([units_of(w) for w in (
        pad_columns(v["a_w1"][0], 0, P), pad_columns(v["a_a1"][0], 64, P), g1[:, :P], pad_columns(g1[:, P:], 0, P))])
    for i, n in enumerate("rkv"):
        out[n] = units_of(v["a_w_rkv"][0, i])
    out["w_o"] = units_of(v["a_w_o"][0])
    lora2 = np.zeros((P, 3, D), np.float32)
    lora2[0:64, 0], lora2[64:, 0] = v["a_w2"][0], v["a_a2"][0]
    lora2[:, 1], lora2[:G_REST, 2] = v["a_g2"][0][:P], v["a_g2"][0][P:]
    out["lora2"] = lora2.reshape(P, 3, DT, P).transpose(2, 0, 1, 3)
    names = {"w0": "a_w0", "a0": "a_a0", "k_k": "a_k_k", "k_a": "a_k_a", "r_k": "a_r_k"}
    out["tvec"] = np.stack([v[names[n]].reshape(DT, P) for n in TILE_VECS], 2)

    def ffn(tag, gate, up, down):
        g, u = units_of(gate), units_of(up)
        gu = np.stack([g, u], 1)
        first = 0
        for p, kt in enumerate(PARTS):
            out[f"{tag}gu{p}"] = gu[first:first + kt].reshape(2 * kt, P, DT, P)
            out[f"{tag}dn{p}"] = units_of(down[first * P:(first + kt) * P])
            first += kt
    for layer in range(2):
        w = v["ffn_w_in"][layer]
        ffn(f"f{layer}", w[:, :FF], w[:, FF:], v["ffn_w_out"][layer])
    ffn("f2", v["w_ffn_gate_2"][0], v["w_ffn_up_2"][0], v["w_ffn_down_2"][0])

    def with_swapped(w):
        return np.concatenate([w, w[:, ROPE // 2:], w[:, :ROPE // 2]], 1)
    down = v["kv_w_down"]
    out["kvd"] = units_of(np.concatenate([down[:, :256], pad_columns(with_swapped(down[:, 256:]), NOPE, P)], 1))
    out["qd"] = units_of(v["q_w_down"][0])
    kv = units_of(v["kv_w_up"])
    qw = v["q_w_up"][0].reshape(384, MLA_HEADS, QK)
    q = np.stack([units_of(np.concatenate([qw[:, h, :NOPE], with_swapped(qw[:, h, NOPE:])], 1))[0]
                  for h in range(MLA_HEADS)])
    for s in range(SLOTS):
        out[f"heads{s}"] = (kv, q)[s % 2][s // 2::2]
    out["o_w"] = units_of(v["o_w"][0])

    w = v["w_in_2"][0]
    order = [h for j in range(4) for h in (j, j + 4)]
    qcols = w[:, 512:1024].reshape(D, 8, HEAD)[:, order].reshape(D, 512)
    out["in"] = units_of(np.concatenate([w[:, :512], qcols, w[:, 1024:1280]], 1))
    attn = v["w_attn_branch_2"][0].reshape(8, HEAD, D)[order].reshape(512, D)
    for s, a in enumerate((w[:, 1280:2304], w[:, 2304:], v["w_pool_branch_2"][0], attn)):
        out[f"mix{s}"] = units_of(a)
    out["pool_w"] = v["w_pool_group_2"][0].transpose(1, 0, 2)
    out["out"] = units_of(v["w_out_2"][0])
    return {k: np.ascontiguousarray(a) for k, a in out.items()}




def kernel(**inputs):
    import concourse.bacc as bacc
    from concourse.bass_utils import run_bass_kernel_spmd

    nc = bacc.Bacc("TRN2", target_bir_lowering=False, num_devices=1)
    arrays = lay_out({k: np.asarray(a) for k, a in inputs.items()})
    dram = {n: nc.dram_tensor(f"in_{n}", a.shape, F32, kind="ExternalInput").ap() for n, a in arrays.items()}
    out_d = nc.dram_tensor("out_t", (P, DT, T), F32, kind="ExternalOutput").ap()
    build(nc, dram, out_d)
    r = run_bass_kernel_spmd(nc, [{f"in_{n}": a for n, a in arrays.items()}], core_ids=[0])
    got = r.results[0]["out_t"]
    return np.ascontiguousarray(got.transpose(1, 0, 2).reshape(1, D, T).transpose(0, 2, 1))
```
